# Optimizing a Trainium2 kernel written in Bass

```python
import jax, jax.numpy as jnp
from jax import lax
import numpy as np

D_MODEL = 1024
BATCH = 1
SEQ = 512
DEPTH = 1
DEC_BATCH = 8
DEC_SEQ = 1
PAST_LEN = 4096
PAGE_SIZE = 128

D_MIX = D_MODEL
D_POOL = D_MIX // 4
D_CONV = D_MIX // 4
D_LRU = D_MIX // 2
D_IN = D_POOL + 2 * D_CONV + 2 * D_LRU
SPLITS = (D_POOL, D_POOL + D_CONV, D_POOL + 2 * D_CONV, D_POOL + 2 * D_CONV + D_LRU)

POOL_WINDOWS = (2, 4, 8, 16)
N_POOL_GROUPS = len(POOL_WINDOWS)
POOL_GROUP = D_POOL // N_POOL_GROUPS
POOL_BUF = max(POOL_WINDOWS) - 1

CONV_WIDTH = 31
CONV_BUF = CONV_WIDTH - 1

LRU_CONV_WIDTH = 4
LRU_BUF = LRU_CONV_WIDTH - 1
LRU_HEADS = 8
LRU_HEAD_DIM = D_LRU // LRU_HEADS
LRU_C = 8.0

N_EXPERTS = 32
TOP_K = 4
D_FF = D_MODEL
SWIGLU_ALPHA = 1.702
SWIGLU_LIMIT = 7.0
MOE_BLOCK = 128

RMS_EPS = 1e-6
LN_EPS = 1e-5

kernel_name = "hybrid_pool_conformer_rglru_moe_decoder_step"

def rms_norm(x, g):
    xf = x.astype(jnp.float32)
    y = xf * lax.rsqrt(jnp.mean(xf * xf, axis=-1, keepdims=True) + RMS_EPS)
    return (y * g.astype(jnp.float32)).astype(x.dtype)

def layer_norm(x, g, b):
    xf = x.astype(jnp.float32)
    mu = jnp.mean(xf, axis=-1, keepdims=True)
    var = jnp.mean(jnp.square(xf - mu), axis=-1, keepdims=True)
    y = (xf - mu) * lax.rsqrt(var + LN_EPS)
    return (y * g.astype(jnp.float32) + b.astype(jnp.float32)).astype(x.dtype)

def causal_depthwise_conv(xp, w, b):
    C = xp.shape[-1]
    y = lax.conv_general_dilated(xp, w[:, None, :].astype(xp.dtype), window_strides=(1,), padding="VALID",
                                 dimension_numbers=("NWC", "WIO", "NWC"), feature_group_count=C)
    return y + b.astype(y.dtype)

def pool_mixer(u, buf, start, w_grp, scale):
    B, S, _ = u.shape
    up = jnp.concatenate([buf.astype(u.dtype), u], axis=1)
    cs = jnp.pad(jnp.cumsum(up.astype(jnp.float32), axis=1), ((0, 0), (1, 0), (0, 0)))
    pos = start + jnp.arange(S)
    hi = cs[:, POOL_BUF + 1:POOL_BUF + 1 + S]
    means = []
    for g, w in enumerate(POOL_WINDOWS):
        ch = slice(g * POOL_GROUP, (g + 1) * POOL_GROUP)
        lo = cs[:, POOL_BUF + 1 - w:POOL_BUF + 1 - w + S, ch]
        cnt = jnp.minimum(pos + 1, w).astype(jnp.float32)[None, :, None]
        means.append((hi[..., ch] - lo) / cnt)
    d = (jnp.concatenate(means, axis=-1) - u.astype(jnp.float32)).reshape(B, S, N_POOL_GROUPS, POOL_GROUP)
    y = jnp.einsum("bsgi,gij->bsgj", d, w_grp.astype(jnp.float32)).reshape(B, S, D_POOL)
    return y * scale.astype(jnp.float32), up[:, -POOL_BUF:]

def conformer_conv(v, gate, buf, dw, db, ln_g, ln_b):
    a = v * jax.nn.sigmoid(gate)
    ap = jnp.concatenate([buf.astype(a.dtype), a], axis=1)
    y = causal_depthwise_conv(ap, dw, db)
    y = jax.nn.silu(layer_norm(y, ln_g, ln_b))
    return y, ap[:, -CONV_BUF:]

def rglru_mixer(xr, gate_br, conv_buf, h0, start, conv_w, conv_b, wa, ba, wx, bx, lam):
    B, S, C = xr.shape
    xp = jnp.concatenate([conv_buf.astype(xr.dtype), xr], axis=1)
    xc = causal_depthwise_conv(xp, conv_w, conv_b).astype(jnp.float32)
    xh = xc.reshape(B, S, LRU_HEADS, LRU_HEAD_DIM)
    r = jax.nn.sigmoid(jnp.einsum("bshi,hij->bshj", xh, wa.astype(jnp.float32)).reshape(B, S, C) + ba)
    i = jax.nn.sigmoid(jnp.einsum("bshi,hij->bshj", xh, wx.astype(jnp.float32)).reshape(B, S, C) + bx)
    log_a = -LRU_C * r * jax.nn.softplus(-lam.astype(jnp.float32))
    a = jnp.exp(log_a)
    mult = jnp.sqrt(-jnp.expm1(2.0 * log_a))
    reset = ((start + jnp.arange(S)) == 0)[None, :, None]
    a = jnp.where(reset, 0.0, a)
    mult = jnp.where(reset, 1.0, mult)
    b = mult * i * xc
    b = b.at[:, 0].add(a[:, 0] * h0.astype(jnp.float32))

    def combine(left, right):
        a1, b1 = left
        a2, b2 = right
        return a1 * a2, a2 * b1 + b2

    _, h = lax.associative_scan(combine, (a, b), axis=1)
    y = h * jax.nn.gelu(gate_br.astype(jnp.float32))
    return y, xp[:, -LRU_BUF:], h[:, -1].astype(h0.dtype)

def moe_ffn(h, router_w, router_b, w_gate, b_gate, w_up, b_up, w_down, b_down):
    B, S, D = h.shape
    xt = h.reshape(-1, D)
    T = xt.shape[0]
    TK = T * TOP_K
    logits = (xt @ router_w + router_b).astype(jnp.float32)
    top_v, top_i = lax.top_k(logits, TOP_K)
    top_w = jax.nn.softmax(top_v, axis=-1)
    flat_e = top_i.reshape(-1).astype(jnp.int32)
    flat_tok = jnp.repeat(jnp.arange(T, dtype=jnp.int32), TOP_K)
    flat_w = top_w.reshape(-1)
    order = jnp.argsort(flat_e, stable=True)
    se = flat_e[order]
    counts = jnp.bincount(flat_e, length=N_EXPERTS).astype(jnp.int32)
    pcounts = (counts + MOE_BLOCK - 1) // MOE_BLOCK * MOE_BLOCK
    starts = jnp.cumsum(counts) - counts
    pends = jnp.cumsum(pcounts)
    pstarts = pends - pcounts
    dest = pstarts[se] + jnp.arange(TK, dtype=jnp.int32) - starts[se]
    n_blocks = -(-TK // MOE_BLOCK) + N_EXPERTS
    n_rows = n_blocks * MOE_BLOCK
    row_tok = jnp.full((n_rows,), T, jnp.int32).at[dest].set(flat_tok[order])
    row_w = jnp.zeros((n_rows,), jnp.float32).at[dest].set(flat_w[order])
    block_e = jnp.minimum(jnp.searchsorted(pends, jnp.arange(n_blocks, dtype=jnp.int32) * MOE_BLOCK, side="right"),
                          N_EXPERTS - 1)
    x_pad = jnp.concatenate([xt, jnp.zeros((1, D), xt.dtype)], axis=0)
    xb = x_pad[row_tok].reshape(n_blocks, MOE_BLOCK, D)

    def expert_block(args):
        xblk, e = args
        g = xblk @ w_gate[e] + b_gate[e]
        u = xblk @ w_up[e] + b_up[e]
        g = jnp.minimum(g, SWIGLU_LIMIT)
        u = jnp.clip(u, -SWIGLU_LIMIT, SWIGLU_LIMIT)
        glu = g * jax.nn.sigmoid(SWIGLU_ALPHA * g)
        return ((u + 1.0) * glu) @ w_down[e] + b_down[e]

    yb = lax.map(expert_block, (xb, block_e)).reshape(n_rows, D)
    y = jax.ops.segment_sum(yb.astype(jnp.float32) * row_w[:, None], row_tok, num_segments=T + 1)[:T]
    return y.astype(h.dtype).reshape(B, S, D)

def trunk_layer(x, c, pool_buf, conv_buf, lru_buf, lru_h, start, p):
    mod = (jax.nn.silu(c) @ p["ada_w"] + p["ada_b"])[:, None, :]
    sh1, sc1, g1, sh2, sc2, g2 = jnp.split(mod, 6, axis=-1)
    h = rms_norm(x, p["norm1_g"]) * (1.0 + sc1) + sh1
    z = h @ p["w_in"]
    u_pool, v_conv, g_conv, x_lru, g_lru = jnp.split(z, SPLITS, axis=-1)
    o_pool, nb_pool = pool_mixer(u_pool, pool_buf, start, p["pool_w"], p["pool_scale"])
    o_conv, nb_conv = conformer_conv(v_conv, g_conv, conv_buf, p["conv_dw"], p["conv_b"],
                                     p["conv_ln_g"], p["conv_ln_b"])
    o_lru, nb_lru, nh_lru = rglru_mixer(x_lru, g_lru, lru_buf, lru_h, start, p["lru_conv_w"], p["lru_conv_b"],
                                        p["lru_wa"], p["lru_ba"], p["lru_wx"], p["lru_bx"], p["lru_lambda"])
    o = jnp.concatenate([o_pool.astype(x.dtype), o_conv.astype(x.dtype), o_lru.astype(x.dtype)], axis=-1)
    x = x + g1 * (o @ p["w_out"])
    h = rms_norm(x, p["norm2_g"]) * (1.0 + sc2) + sh2
    x = x + g2 * moe_ffn(h, p["router_w"], p["router_b"], p["moe_w_gate"], p["moe_b_gate"],
                         p["moe_w_up"], p["moe_b_up"], p["moe_w_down"], p["moe_b_down"])
    return x, nb_pool, nb_conv, nb_lru, nh_lru

def setup_inputs(seed: int = 0) -> dict:
    key = jax.random.key(seed)
    ks = iter(jax.random.split(key, 40))
    f32 = jnp.float32

    def nrm(shape, scale):
        return jax.random.normal(next(ks), shape, f32) * scale

    def gain(shape):
        return 1.0 + 0.05 * jax.random.normal(next(ks), shape, f32)

    a0 = jax.random.uniform(next(ks), (DEPTH, D_LRU), f32, 0.9, 0.999)
    a_base = a0 ** (1.0 / LRU_C)
    lam = jnp.log(a_base) - jnp.log1p(-a_base)
    return {
        "x_prompt": nrm((BATCH, SEQ, D_MODEL), 1.0),
        "x_sample": nrm((DEC_BATCH, DEC_SEQ, D_MODEL), 1.0),
        "state_pool": nrm((DEPTH, DEC_BATCH, POOL_BUF, D_POOL), 1.0),
        "state_conv": nrm((DEPTH, DEC_BATCH, CONV_BUF, D_CONV), 0.5),
        "state_lru_conv": nrm((DEPTH, DEC_BATCH, LRU_BUF, D_LRU), 1.0),
        "state_lru_h": nrm((DEPTH, DEC_BATCH, D_LRU), 0.5),
        "c_prompt": nrm((BATCH, D_MODEL), 1.0),
        "c_sample": nrm((DEC_BATCH, D_MODEL), 1.0),
        "ada_w": nrm((DEPTH, D_MODEL, 6 * D_MODEL), 0.5 * D_MODEL ** -0.5),
        "ada_b": nrm((DEPTH, 6 * D_MODEL), 0.02),
        "norm1_g": gain((DEPTH, D_MODEL)),
        "w_in": nrm((DEPTH, D_MODEL, D_IN), D_MODEL ** -0.5),
        "pool_w": nrm((DEPTH, N_POOL_GROUPS, POOL_GROUP, POOL_GROUP), POOL_GROUP ** -0.5),
        "pool_scale": gain((DEPTH, D_POOL)),
        "conv_dw": nrm((DEPTH, CONV_WIDTH, D_CONV), CONV_WIDTH ** -0.5),
        "conv_b": nrm((DEPTH, D_CONV), 0.02),
        "conv_ln_g": gain((DEPTH, D_CONV)),
        "conv_ln_b": nrm((DEPTH, D_CONV), 0.02),
        "lru_conv_w": nrm((DEPTH, LRU_CONV_WIDTH, D_LRU), LRU_CONV_WIDTH ** -0.5),
        "lru_conv_b": nrm((DEPTH, D_LRU), 0.02),
        "lru_wa": nrm((DEPTH, LRU_HEADS, LRU_HEAD_DIM, LRU_HEAD_DIM), LRU_HEAD_DIM ** -0.5),
        "lru_ba": nrm((DEPTH, D_LRU), 0.02),
        "lru_wx": nrm((DEPTH, LRU_HEADS, LRU_HEAD_DIM, LRU_HEAD_DIM), LRU_HEAD_DIM ** -0.5),
        "lru_bx": nrm((DEPTH, D_LRU), 0.02),
        "lru_lambda": lam,
        "w_out": nrm((DEPTH, D_MIX, D_MODEL), D_MIX ** -0.5),
        "norm2_g": gain((DEPTH, D_MODEL)),
        "router_w": nrm((DEPTH, D_MODEL, N_EXPERTS), D_MODEL ** -0.5),
        "router_b": nrm((DEPTH, N_EXPERTS), 0.01),
        "moe_w_gate": nrm((DEPTH, N_EXPERTS, D_MODEL, D_FF), D_MODEL ** -0.5),
        "moe_b_gate": nrm((DEPTH, N_EXPERTS, D_FF), 0.02),
        "moe_w_up": nrm((DEPTH, N_EXPERTS, D_MODEL, D_FF), D_MODEL ** -0.5),
        "moe_b_up": nrm((DEPTH, N_EXPERTS, D_FF), 0.02),
        "moe_w_down": nrm((DEPTH, N_EXPERTS, D_FF, D_MODEL), D_FF ** -0.5),
        "moe_b_down": nrm((DEPTH, N_EXPERTS, D_MODEL), 0.02),
        "final_g": gain((D_MODEL,)),
    }

def reference(x_prompt, x_sample, state_pool, state_conv, state_lru_conv, state_lru_h, c_prompt, c_sample,
              ada_w, ada_b, norm1_g, w_in, pool_w, pool_scale, conv_dw, conv_b, conv_ln_g, conv_ln_b,
              lru_conv_w, lru_conv_b, lru_wa, lru_ba, lru_wx, lru_bx, lru_lambda, w_out, norm2_g,
              router_w, router_b, moe_w_gate, moe_b_gate, moe_w_up, moe_b_up, moe_w_down, moe_b_down, final_g):
    layers = [dict(ada_w=ada_w[l], ada_b=ada_b[l], norm1_g=norm1_g[l], w_in=w_in[l], pool_w=pool_w[l],
                   pool_scale=pool_scale[l], conv_dw=conv_dw[l], conv_b=conv_b[l], conv_ln_g=conv_ln_g[l],
                   conv_ln_b=conv_ln_b[l], lru_conv_w=lru_conv_w[l], lru_conv_b=lru_conv_b[l], lru_wa=lru_wa[l],
                   lru_ba=lru_ba[l], lru_wx=lru_wx[l], lru_bx=lru_bx[l], lru_lambda=lru_lambda[l], w_out=w_out[l],
                   norm2_g=norm2_g[l], router_w=router_w[l], router_b=router_b[l], moe_w_gate=moe_w_gate[l],
                   moe_b_gate=moe_b_gate[l], moe_w_up=moe_w_up[l], moe_b_up=moe_b_up[l],
                   moe_w_down=moe_w_down[l], moe_b_down=moe_b_down[l])
              for l in range(DEPTH)]

    def run(x, c, pool_s, conv_s, lru_conv_s, lru_h_s, start):
        np_, nc_, nl_, nh_ = [], [], [], []
        for l in range(DEPTH):
            x, nb_pool, nb_conv, nb_lru, nh_lru = trunk_layer(x, c, pool_s[l], conv_s[l], lru_conv_s[l],
                                                               lru_h_s[l], start, layers[l])
            np_.append(nb_pool)
            nc_.append(nb_conv)
            nl_.append(nb_lru)
            nh_.append(nh_lru)
        return rms_norm(x, final_g), jnp.stack(np_), jnp.stack(nc_), jnp.stack(nl_), jnp.stack(nh_)

    B = x_prompt.shape[0]
    dt = x_prompt.dtype
    y_prompt, pool_p, conv_p, lruc_p, lruh_p = run(
        x_prompt, c_prompt,
        jnp.zeros((DEPTH, B, POOL_BUF, D_POOL), dt), jnp.zeros((DEPTH, B, CONV_BUF, D_CONV), dt),
        jnp.zeros((DEPTH, B, LRU_BUF, D_LRU), dt), jnp.zeros((DEPTH, B, D_LRU), dt), 0)
    y_sample, pool_s, conv_s, lruc_s, lruh_s = run(
        x_sample, c_sample, state_pool, state_conv, state_lru_conv, state_lru_h, PAST_LEN)
    return (y_prompt, y_sample, pool_p, conv_p, lruc_p, lruh_p, pool_s, conv_s, lruc_s, lruh_s)


_drawn_inputs = setup_inputs


def setup_inputs(seed=0):
    import zlib

    import numpy as np

    out = dict(_drawn_inputs(seed))
    spreads = {}
    factors = {'pool_scale': 4.8,
     'conv_b': 8.0,
     'conv_ln_g': 5.608,
     'conv_ln_b': 27.606,
     'lru_ba': 8.0,
     'lru_bx': 6.858,
     'router_b': 14.787,
     'moe_b_gate': 8.0,
     'moe_b_up': 28.909,
     'moe_b_down': 24.771,
     'norm2_g': 2.811}
    for name, (base, spread) in spreads.items():
        noise = np.random.default_rng([zlib.crc32(name.encode()), seed]).standard_normal(out[name].shape)
        drawn = base * np.exp(spread * noise) if base else spread * noise
        out[name] = __import__('jax').numpy.asarray(drawn.astype(out[name].dtype))
    for name, factor in factors.items():
        out[name] = (out[name] * factor).astype(out[name].dtype)
    return out
```

```python
from contextlib import ExitStack

import concourse.bass as bass
from concourse import mybir

F32 = mybir.dt.float32
F32R = mybir.dt.float32r
I32 = mybir.dt.int32
U32 = mybir.dt.uint32
ALU = mybir.AluOpType
ACT = mybir.ActivationFunctionType
AX = mybir.AxisListType

P = 128
D = 1024
KC = D // P
SEQ, NB = 512, 8
TOK = SEQ + NB
TT = SEQ // P + 1
ROWS = [P] * (TT - 1) + [NB]
NC = NB + 1
D_POOL, D_CONV, D_LRU = 256, 256, 512
D_IN = D_POOL + 2 * D_CONV + 2 * D_LRU
PB, CB, LB = 15, 30, 3
CW, LW = 31, 4
E, K, DFF = 32, 4, 1024
XTRA = 16
TASKS = E + XTRA
PAIRS_MAIN, PAIRS = E // 2, TASKS // 2

CH = 2048
R_LO, R_HI = 8, 4
ADA_A = 8
WIN = D_IN // 256
ADA_B = 16
WOUT = 4
C_WIN, C_ADAB, C_WOUT = ADA_A, ADA_A + WIN, ADA_A + WIN + ADA_B
C_MOE = C_WOUT + WOUT
PER_TASK = 12
PER_PAIR = 2 * PER_TASK
LO_POOL = (4, 9)
PRM_LOADS, BC_LOADS = 22, 9
WOUT_AT = {5: (0,), 6: (1, 2), 7: (3,)}
WIN_ORDER = [1, 2, 3, 4, 0, 5, 6]

RMS_EPS, LN_EPS = 1e-6, 1e-5


def trunk_program(nc, x_prompt, x_sample, state_pool, state_conv, state_lru_conv, state_lru_h, c_prompt, c_sample,
                  ada_w, ada_b, norm1_g, w_in, pool_w, pool_scale, conv_dw, conv_b, conv_ln_g, conv_ln_b,
                  lru_conv_w, lru_conv_b, lru_wa, lru_ba, lru_wx, lru_bx, lru_lambda, w_out, norm2_g,
                  router_w, router_b, moe_w_gate, moe_b_gate, moe_w_up, moe_b_up, moe_w_down, moe_b_down, final_g,
                  y_prompt, y_sample, pool_p, conv_p, lruc_p, lruh_p, pool_s, conv_s, lruc_s, lruh_s):
    base = -(-nc.sbuf_base // 32) * 32
    top = nc.sbuf_usable_end

    def place(start, *items):
        out, at = [], base + start
        for name, shape, dt in items:
            out.append(nc.alloc_sbuf_tensor_at(name, shape, dt, offset=at))
            n = 4
            for s in shape[1:]:
                n *= s
            at += -(-n // 32) * 32
        assert at <= top, (name, at, top)
        return out, at - base

    (w_lo, w_hi), X0 = place(0, ("w_lo", [P, R_LO, CH], F32R), ("w_hi", [P, R_HI, CH], F32R))
    (raw,), _ = place(0, ("raw", [P, R_LO, CH], F32))
    (ident, tri, ones, iota1, pmod, prmT, etab, bsel, cols, task_i, cT, adab), XC = place(
        X0, ("ident", [P, P], F32), ("tri", [P, P], F32), ("ones", [P, P], F32), ("iota1", [P, P], F32),
        ("pmod", [P, P], F32), ("prmT", [P, 112], F32), ("etab", [P, TASKS + 2], F32), ("bsel", [12, 12, NC], F32),
        ("cols", [P, 64], F32), ("task_i", [1, XTRA + 1], I32), ("cT", [P, KC, NC], F32),
        ("adab", [12, 512], F32))
    (pp, choice, wts, rows_i, wfull), PPEND = place(
        XC - 2048, ("pp", [P, TT, TASKS + 2], F32), ("choice", [P, TT, 4], F32), ("wts", [P, TT, 4], F32),
        ("rows_i", [P, TT, 4], I32), ("wfull", [P, TT, E], F32))
    assert PPEND <= XC
    A0 = XC
    (hT_hi, hT_lo), W0 = place(A0, ("hT_hi", [P, KC, TOK], F32R), ("hT_lo", [P, KC, TOK], F32R))
    oT_hi, oT_lo = hT_hi, hT_lo
    (bias_raw, scr1), _ = place(A0, ("bias_raw", [2 * E, 2 * DFF], F32), ("scr1", [P, D], F32))
    (W,), Z0 = place(W0, ("W", [P, 10, TOK], F32))
    (x1,), _ = place(W0, ("x1", [P, TT, D], F32))
    PW = PB + SEQ
    (tail,), _ = place(W0, ("tail", [38, 3 * 512], F32))
    (modA, cv, lr, ng, c_all, st_pool, st_conv, st_lru, st_h, hf, mT, hs), Z1 = place(
        Z0, ("modA", [NC, 2048], F32), ("cv", [35, D_CONV], F32), ("lr", [8, D_LRU], F32), ("ng", [1, D], F32),
        ("c_all", [NC, D], F32), ("st_pool", [NB * PB, D_POOL], F32),
        ("st_conv", [NB * PB, 2, D_CONV], F32), ("st_lru", [NB * LB, D_LRU], F32), ("st_h", [NB, D_LRU], F32),
        ("hf", [P, 2, TOK], F32), ("mT", [P, 2 * KC, NC], F32), ("hs", [P, KC, NB], F32))
    (u_pool, a_conv, v_conv, sg_conv, x_lru, g_lru), B0 = place(
        Z0, ("u_pool", [P, 2, PB + TOK], F32), ("a_conv", [P, 2, CB + TOK], F32), ("v_conv", [P, 2, TOK], F32),
        ("sg_conv", [P, 2, TOK], F32), ("x_lru", [P, 4, LB + TOK], F32), ("g_lru", [P, 4, TOK], F32))
    (bd_pool, bd_a, bd_x, modst, sT_conv, sT_pool, sT_lru, sT_h, h_tail, rc16,
     head, win_s), B1 = place(
        B0, ("bd_pool", [P, 2, P], F32), ("bd_a", [P, 4, P], F32), ("bd_x", [P, 4, P], F32), ("modst", [NC, 512], F32),
        ("sT_conv", [P, 2, NB * CB], F32), ("sT_pool", [P, 2, NB * PB], F32), ("sT_lru", [P, 4, NB * LB], F32),
        ("sT_h", [P, 4, NB], F32), ("h_tail", [P, 4, NB + 1], F32), ("rc16", [P, 2, 16], F32),
        ("head", [P, 16], F32), ("win_s", [P, 2, NB], F32))
    B2 = top - base - 8192 - 32
    B2 -= (base + B2) % 32
    (btab,), _ = place(B2, ("btab", [P, 2 * DFF], F32R))
    assert Z1 <= B0 and B1 <= B2, (Z1, B0, B1, B2)
    (h2,), N0 = place(A0, ("h2", [P, TT, 2, D], F32R))
    (x2, g1b, g1s, sh2b, A2b, sh2s, A2s, h2f, rw, h2T, sq2t, rbb, zeros), N1 = place(
        N0, ("x2", [P, TT, D], F32), ("g1b", [P, D], F32), ("g1s", [NB, D], F32), ("sh2b", [P, D], F32),
        ("A2b", [P, D], F32), ("sh2s", [NB, D], F32), ("A2s", [NB, D], F32), ("h2f", [P, D], F32),
        ("rw", [P, KC, E], F32), ("h2T", [P, KC, P], F32), ("sq2t", [P, 512], F32), ("rbb", [P, E], F32), ("zeros", [P, P], F32))
    assert N1 <= B2, (N1, B2)
    R0 = N0 + 16384 + 5120 + 1024
    (logit, hot, mask, rowm, tmpE4, v8, i8, i8f, smallE, posT, selX, xcol, extras, n2b), R1 = place(
        R0, ("logit", [P, TT, E], F32), ("hot", [P, TT, 4, E], F32), ("mask", [P, TT, E], F32),
        ("rowm", [P, TT, E], F32), ("tmpE4", [P, K, E], F32), ("v8", [P, TT, 8], F32), ("i8", [P, TT, 8], U32),
        ("i8f", [P, TT, 8], F32), ("smallE", [P, 8, E], F32), ("posT", [E, TT, P], F32), ("selX", [E, 4, XTRA], F32),
        ("xcol", [E, 16], F32), ("extras", [1, 4], F32), ("n2b", [1, 4], F32))
    assert R1 <= N0 + TT * D * 4 + 3 * 4096, R1
    (xg, gat, sel, t_g, sig, ucl, actv, aT_hi, aT_lo, yst), M1 = place(
        N0, ("xg", [P, KC, 2, 2 * P], F32R), ("gat", [P, TT, 2 * P], F32R), ("sel", [P, 2, P], F32R),
        ("t_g", [P, 2, 512], F32), ("sig", [P, 2, 512], F32), ("ucl", [P, 2, 512], F32), ("actv", [P, 2, 512], F32),
        ("aT_hi", [P, 2, 4, P], F32R), ("aT_lo", [P, 2, 4, P], F32R), ("yst", [P, 2, D], F32))
    assert M1 <= B2, (M1, B2)
    (x2e, g2b, g2s, fgb, yrow, acc, out_t, WT, bdn, sq_e), _ = place(
        A0, ("x2e", [P, TT, D], F32), ("g2b", [P, D], F32), ("g2s", [NB, D], F32), ("fgb", [P, D], F32),
        ("yrow", [P, 2, K, D], F32), ("acc", [P, 2, D], F32), ("out_t", [P, 2, D], F32), ("WT", [E, TT, P], F32),
        ("bdn", [E, D], F32), ("sq_e", [P, D], F32))

    mod_d = nc.dram_tensor("mod_scratch", (NC, 4 * D), F32).ap()
    x2_d = nc.dram_tensor("x2_scratch", (TT * P, D), F32).ap()
    y_d = nc.dram_tensor("y_scratch", (TASKS * P, D), F32).ap()

    ctx = ExitStack()
    with ctx:
        psum = ctx.enter_context(nc.psum_tensor("psum", [P, 8, 512], F32))
        bk = [psum[:, i, :] for i in range(8)]

        def pair(i):
            return psum[:, i:i + 2, 0:TOK // 2]

        def two(ap):
            return ap.rearrange("p (h n) -> p h n", h=2)

        def sem(name):
            return ctx.enter_context(nc.semaphore(name))

        raw_full = [sem(f"raw_full{i}") for i in range(R_LO)]
        hi_done, lo_done, lo_pool, chunk_used = sem("hi_done"), sem("lo_done"), sem("lo_pool"), sem("chunk_used")
        adab_loaded, bias_loaded = sem("adab_loaded"), sem("bias_loaded")
        c_loaded, x_loaded, prm_loaded, bd_zero = sem("c_loaded"), sem("x_loaded"), sem("prm_loaded"), sem("bd_zero")
        consts_done, pool_chain, dve_chain, act_chain = (
            sem("consts_done"), sem("pool_chain"), sem("dve_chain"), sem("act_chain"))
        cT_ps, cT_done, prm_ps, prm_done, st_ps, st_done = (
            sem("cT_ps"), sem("cT_done"), sem("prm_ps"), sem("prm_done"), sem("st_ps"), sem("st_done"))
        pads_done, silu_done = sem("pads_done"), sem("silu_done")
        ada_ev, modT_ps, modT_done = sem("ada_ev"), sem("modT_ps"), sem("modT_done")
        ss1_done, rms1_done, xn_done = sem("ss1_done"), sem("rms1_done"), sem("xn_done")
        xT_ps, h1_act, hT_done, xs_ps = sem("xT_ps"), sem("h1_act"), sem("hT_done"), sem("xs_ps")
        z_ps, z_ev, u_ev = sem("z_ps"), sem("z_ev"), sem("u_ev")
        xc_done, gates_ps, gates_done, lru_act, lru_dve, lru_sqrt = (
            sem("xc_done"), sem("gates_ps"), sem("gates_done"), sem("lru_act"), sem("lru_dve"), sem("lru_sqrt"))
        mix_done, sq_done, centered, ln_var, ln_sd, ln_pre, ln_sig = (
            sem("mix_done"), sem("sq_done"), sem("centered"), sem("ln_var"), sem("ln_sd"), sem("ln_pre"), sem("ln_sig"))
        pool_in, pool_ps, oT_done = sem("pool_in"), sem("pool_ps"), sem("oT_done")
        conv_done, tail_ps, pool_d_done, tail_out, old_rows = (
            sem("conv_done"), sem("tail_ps"), sem("pool_d_done"), sem("tail_out"), sem("old_rows"))
        mod_out, bc_loaded = sem("mod_out"), sem("bc_loaded")
        x2_loaded, wo_ps, x2_done, x2_spill = sem("x2_loaded"), sem("wo_ps"), sem("x2_done"), sem("x2_spill")
        ss2_done, sd2_done, h2_ready, h2hi_done, h2_done, h2T_ps, h2T_done, logit_ps, a2_raw = (
            sem("ss2_done"), sem("sd2_done"), sem("h2_ready"), sem("h2hi_done"), sem("h2_done"), sem("h2T_ps"),
            sem("h2T_done"), sem("logit_ps"), sem("a2_raw"))
        exp_in, exp_done, o_split, mu_ps, pp_done, posT_ps, posT_done, xe_done, base_ps, selX_done, xtab_ps = (
            sem("exp_in"), sem("exp_done"), sem("o_split"), sem("mu_ps"), sem("pp_done"), sem("posT_ps"),
            sem("posT_done"), sem("xe_done"), sem("base_ps"), sem("selX_done"), sem("xtab_ps"))
        tables_done = sem("tables_done")
        h2_zero, tail_read, y_zero = sem("h2_zero"), sem("tail_read"), sem("y_zero")
        gat_done, xg_ps, xg_a, xg_d, sel_done = (
            sem("gat_done"), sem("xg_ps"), sem("xg_a"), sem("xg_d"), sem("sel_done"))
        tg_done, sig_done, act_done, aT_ps, aThi_done, aTlo_done = (
            sem("tg_done"), sem("sig_done"), sem("act_done"), sem("aT_ps"), sem("aThi_done"), sem("aTlo_done"))
        y_a, y_v = sem("y_a"), sem("y_v")
        y_out = [sem("y_out0"), sem("y_out1")]
        moe_chain = sem("moe_chain")
        rows_ready, e_loaded, WT_ps, WT_done, yb_ps, fetched, fetched2, acc_done, out_ready, out_sent = (
            sem("rows_ready"), sem("e_loaded"), sem("WT_ps"), sem("WT_done"), sem("yb_ps"), sem("fetched0"),
            sem("fetched1"), sem("acc_done"), sem("out_ready"), sem("out_sent"))
        sse_done, sde_done, yb_read = sem("sse_done"), sem("sde_done"), sem("yb_read")
        out_sent2 = sem("out_sent2")

        def cvp(row, m):
            return prmT[:, 35 * m + row:35 * m + row + 1]

        def lrp(row, m):
            return prmT[:, 70 + 8 * m + row:70 + 8 * m + row + 1]

        N1G = 102
        EPS, LNEPS, SSQ, RSTD, SP8, SAVE, SSQ2, SD2, WCOL = 0, 1, 2, 8, 14, 30, 32, 44, 50

        def halves(ap):
            return ap.rearrange("p (k n) -> p k n", k=4)

        def wide(ap):
            return ap.rearrange("p (k n) -> p k n", k=KC)

        def z_wait(eng, z):
            if z % 2:
                eng.wait_ge(chunk_used, C_WIN + z // 2 + 1)
            else:
                eng.wait_ge(z_ps, z // 2 + 1)

        def split_no(c):
            return c - ADA_A if c < C_ADAB else c - ADA_A - ADA_B

        def hi_slot(c):
            return w_hi[:, split_no(c) % R_HI, :]

        def lo_wait(eng, s, c):
            a, i = (c - C_MOE) // PER_TASK, (c - C_MOE) % PER_TASK
            by_pool = a * len(LO_POOL) + sum(j <= i for j in LO_POOL)
            if i in LO_POOL:
                eng.wait_ge(lo_pool, s * (2 * len(LO_POOL)) + by_pool)
            else:
                eng.wait_ge(lo_done, s * (PER_PAIR - 2 * len(LO_POOL)) + (split_no(c) + 1 - by_pool))

        def wo_wait(eng, n, t):
            if t == TT - 1:
                eng.wait_ge(chunk_used, C_WOUT + 2 * n + 2)
            else:
                eng.wait_ge(wo_ps, (TT - 1) * n + t + 1)

        block = ctx.enter_context(nc.Block())

        @block.sync
        def _(sp):
            sp.dma_start(c_all[0:NB, :], c_sample).then_inc(c_loaded, 16)
            sp.dma_start(c_all[NB:NC, :], c_prompt).then_inc(c_loaded, 16)
            sp.dma_start(adab[:, :], ada_b[0].rearrange("(n c) -> n c", c=512)).then_inc(adab_loaded, 16)

            loads = [0]

            def load_p(dst, src):
                sp.dma_start(dst, src).then_inc(prm_loaded, 16)
                loads[0] += 1

            def small_loads():
                load_p(cv[0:CW, :], conv_dw[0])
                load_p(cv[31:32, :], conv_b)
                load_p(cv[32:33, :], conv_ln_g)
                load_p(cv[33:34, :], conv_ln_b)
                load_p(cv[34:35, :], pool_scale)
                load_p(lr[0:LW, :], lru_conv_w[0])
                load_p(lr[4:5, :], lru_conv_b)
                load_p(lr[5:6, :], lru_ba)
                load_p(lr[6:7, :], lru_bx)
                load_p(lr[7:8, :], lru_lambda)
                load_p(ng[:, :], norm1_g)
                load_p(st_pool[:, :], state_pool[0].rearrange("b r c -> (b r) c"))
                for a in range(2):
                    load_p(st_conv[:, a, :], state_conv[0, 4 * a:4 * a + 4].rearrange("b r c -> (b r) c"))
                load_p(st_lru[:, :], state_lru_conv[0].rearrange("b r c -> (b r) c"))
                load_p(st_h[:, :], state_lru_h[0])
                sp.wait_ge(bd_zero, 1)
                for j in range(2):
                    q = slice(64 * j, 64 * j + 64)
                    load_p(bd_pool[q, :, q], pool_w[0].rearrange("(m j) i o -> j i m o", j=2)[j])
                    load_p(bd_a[q, :, q], lru_wa[0].rearrange("(m j) i o -> j i m o", j=2)[j])
                    load_p(bd_x[q, :, q], lru_wx[0].rearrange("(m j) i o -> j i m o", j=2)[j])
                assert loads[0] == PRM_LOADS

            def load(c, src, s=None):
                slot = c % R_LO
                if s is None:
                    if c >= R_LO:
                        sp.wait_ge(chunk_used, c - R_LO + 1)
                else:
                    sp.wait_ge(chunk_used, s * PER_PAIR + (c - R_LO + 1))
                sp.dma_start(raw[:, slot, :].rearrange("p (k n) -> p k n", k=src.shape[1]), src)\
                    .then_inc(raw_full[slot], 16)

            ada = ada_w[0].rearrange("(k p) n -> p k n", p=P)
            win = w_in[0].rearrange("(k p) n -> p k n", p=P)
            wout = w_out[0].rearrange("(k p) n -> p k n", p=P)
            for c in range(ADA_A):
                load(c, ada[:, 4 * (c % 2):4 * (c % 2) + 4, (c // 2) * 512:(c // 2 + 1) * 512])
                if c == 2:
                    for r in range(2):
                        sp.dma_start(bias_raw[E * r:E * r + E, 0:DFF], moe_b_gate[0]).then_inc(bias_loaded, 16)
                        sp.dma_start(bias_raw[E * r:E * r + E, DFF:2 * DFF], moe_b_up[0]).then_inc(bias_loaded, 16)
                if c == 3:
                    sp.dma_start(x1[:, 0:TT - 1, :], x_prompt[0].rearrange("(t p) d -> p t d", p=P))\
                        .then_inc(x_loaded, 16)
                    sp.dma_start(x1[0:NB, TT - 1, :], x_sample.rearrange("b s d -> (b s) d")).then_inc(x_loaded, 16)
            small_loads()
            for i, w in enumerate(WIN_ORDER):
                load(C_WIN + i, win[:, :, 256 * w:256 * w + 256])
            for c in range(ADA_B):
                n = 4 + c // 2
                load(C_ADAB + c, ada[:, 4 * (c % 2):4 * (c % 2) + 4, n * 512:(n + 1) * 512])
            for c in range(WOUT):
                load(C_WOUT + c, wout[:, 4 * (c % 2):4 * (c % 2) + 4, (c // 2) * 512:(c // 2 + 1) * 512])

            def task(e, off, s):
                mats = [m[0, e].rearrange("(k p) n -> p k n", p=P) if isinstance(e, int) else
                        m[0, bass.ds(e, 1)].rearrange("o (k p) n -> p (o k) n", p=P)
                        for m in (moe_w_gate, moe_w_up, moe_w_down)]
                c = C_MOE + off
                for n in range(2):
                    for m in range(2):
                        for kh in range(2):
                            load(c, mats[m][:, 4 * kh:4 * kh + 4, 512 * n:512 * n + 512], s)
                            c += 1
                for kh in range(2):
                    for n in range(2):
                        load(c, mats[2][:, 4 * kh:4 * kh + 4, 512 * n:512 * n + 512], s)
                        c += 1

            with sp.Fori(0, PAIRS_MAIN) as s:
                task(s * 2, 0, s)
                task(s * 2 + 1, PER_TASK, s)
            sp.wait_ge(tables_done, 1)
            n_pairs = sp.value_load(task_i[0:1, XTRA:XTRA + 1], min_val=PAIRS_MAIN, max_val=PAIRS)
            with sp.Fori(PAIRS_MAIN, PAIRS) as s:
                with sp.If(s < n_pairs):
                    for a in range(2):
                        e = sp.value_load(task_i[0:1, bass.ds(s * 2 + (a - E), 1)], min_val=0, max_val=E - 1)
                        task(e, a * PER_TASK, s)

            for t in range(TT):
                sp.wait_ge(out_ready, t + 1)
                dst = y_prompt[0].rearrange("(t p) d -> t p d", p=P)[t] if t < TT - 1 else \
                    y_sample.rearrange("b s d -> (b s) d")
                sp.dma_start(dst, out_t[0:ROWS[t], t % 2, :]).then_inc([out_sent, out_sent2][t % 2], 16)
            sp.wait_ge(out_sent, 48)
            sp.wait_ge(out_sent2, 32)

        @block.gpsimd
        def _(g):
            n_chain = [0]

            def link(ins):
                n_chain[0] += 1
                ins.then_inc(pool_chain, 1)
                g.wait_ge(pool_chain, n_chain[0])

            g.memset(bd_pool[:, :, :], 0.0)
            g.memset(bd_a[:, :, :], 0.0)
            g.memset(bd_x[:, :, :], 0.0).then_inc(bd_zero, 1)
            g.memset(ones[:, :], 1.0)
            g.memset(tri[:, :], 1.0)
            g.memset(bsel[:, :, :], 1.0)
            link(g.memset(cols[:, EPS:EPS + 1], RMS_EPS))
            link(g.memset(cols[:, LNEPS:LNEPS + 1], LN_EPS))
            link(g.memset(cols[:, SSQ:SSQ + 6], 1.0))
            for j, w in ((0, 2), (1, 8)):
                link(g.memset(cols[0:64, WCOL + j:WCOL + j + 1], 1.0 / w))
                link(g.memset(cols[64:P, WCOL + j:WCOL + j + 1], 0.5 / w))
                link(g.memset(cols[0:64, WCOL + 2 + j:WCOL + 3 + j], float(w)))
                link(g.memset(cols[64:P, WCOL + 2 + j:WCOL + 3 + j], 2.0 * w))
            g.iota(iota1[:, :], pattern=[[1, P]], base=1, channel_multiplier=0, allow_small_or_imprecise_dtypes=True)
            link(g.iota(etab[:, 0:TASKS], pattern=[[1, TASKS]], base=0, channel_multiplier=0,
                        allow_small_or_imprecise_dtypes=True))
            link(g.iota(pmod[0:32, :], pattern=[[0, P]], base=0, channel_multiplier=1, allow_small_or_imprecise_dtypes=True))
            link(g.iota(pmod[32:64, :], pattern=[[0, P]], base=0, channel_multiplier=1, allow_small_or_imprecise_dtypes=True))
            link(g.memset(pmod[64:P, :], -1.0))
            link(g.memset(ident[:, :], 0.0))
            link(g.affine_select(out=ident[:, :], in_=ident[:, :], compare_op=ALU.not_equal, fill=1.0, base=0,
                                 pattern=[[-1, P]], channel_multiplier=1))
            link(g.affine_select(out=tri[:, :], in_=tri[:, :], compare_op=ALU.is_gt, fill=0.0, base=0,
                                 pattern=[[1, P]], channel_multiplier=-1))
            link(g.affine_select(out=bsel[:, :, :], in_=bsel[:, :, :], compare_op=ALU.is_equal, fill=0.0, base=0,
                                 pattern=[[-1, 12], [0, NC]], channel_multiplier=1))
            g.memset(etab[:, TASKS:TASKS + 2], 0.0).then_inc(consts_done, 1)

            g.dma_start(pool_s[0, :, 0:PB - 1, :], state_pool[0, :, 1:PB, :]).then_inc(old_rows, 16)
            g.dma_start(conv_s[0, :, 0:CB - 1, :], state_conv[0, :, 1:CB, :]).then_inc(old_rows, 16)
            g.dma_start(lruc_s[0, :, 0:LB - 1, :], state_lru_conv[0, :, 1:LB, :]).then_inc(old_rows, 16)

            g.wait_ge(z_ps, 1)
            g.memset(u_pool[:, :, 0:PB], 0.0)
            g.memset(a_conv[:, :, 0:CB], 0.0)
            g.memset(x_lru[:, :, 0:LB], 0.0).then_inc(pads_done, 1)

            A, B = v_conv, sg_conv
            tt = g.tensor_tensor
            g.wait_ge(mix_done, 1)
            g.wait_ge(u_ev, 2)
            g.wait_ge(pads_done, 1)
            link(tt(A[:, :, 0:SEQ], u_pool[:, :, PB:PB + SEQ], u_pool[:, :, PB - 1:PB + SEQ - 1], ALU.add))

            def double(dst, src, q, m, w):
                link(g.tensor_copy(dst[q, m, 0:w], src[q, m, 0:w]))
                link(tt(dst[q, m, w:SEQ], src[q, m, w:SEQ], src[q, m, 0:SEQ - w], ALU.add))

            top_, low_, all_ = slice(0, 64), slice(64, P), slice(0, P)
            double(B, A, low_, 0, 2)
            double(B, A, all_, 1, 2)
            double(A, B, all_, 1, 4)
            double(B, A, low_, 1, 8)
            for q, m, s in ((top_, 0, A), (low_, 0, B), (top_, 1, A), (low_, 1, B)):
                inv = cols[q, WCOL + m:WCOL + m + 1]
                link(tt(head[q, :], s[q, m, 0:16], rc16[q, m, :], ALU.mult))
                link(g.tensor_scalar(A[q, m, 0:SEQ], s[q, m, 0:SEQ], inv, None, ALU.mult))
                link(g.tensor_copy(A[q, m, 0:16], head[q, :]))
                link(g.tensor_scalar(A[q, m, SEQ:TOK], win_s[q, m, :], inv, None, ALU.mult))
                link(tt(A[q, m, :], A[q, m, :], u_pool[q, m, PB:PB + TOK], ALU.subtract))
            g.memset(head[:, :], 0.0).then_inc(pool_d_done, 1)

            def lru_out(m):
                j = m % 2
                g.wait_ge(mix_done, m + 2)
                g.wait_ge(z_ev, m + 9)
                link(tt(W[:, 4 + j, :], W[:, 2 + j, :], g_lru[:, m, :], ALU.mult))
                link(g.tensor_copy(oT_hi[:, 4 + m, :], W[:, 4 + j, :]))
                tt(oT_lo[:, 4 + m, :], W[:, 4 + j, :], oT_hi[:, 4 + m, :].bitcast(F32), ALU.subtract)\
                    .then_inc(oT_done, 1)

            z_wait(g, 13)
            lru_out(0)
            lru_out(1)
            lru_out(2)
            lru_out(3)
            g.wait_ge(mod_out, 128)
            g.wait_ge(tail_out, 128)
            g.wait_ge(o_split, 4)
            g.wait_ge(oT_done, 4)
            g.dma_start(x2[:, 0:TT - 1, :], x_prompt[0].rearrange("(t p) d -> p t d", p=P)).then_inc(x2_loaded, 16)
            g.dma_start(x2[0:NB, TT - 1, :], x_sample.rearrange("b s d -> (b s) d")).then_inc(x2_loaded, 16)
            for dst, src in ((g1b, 0), (sh2b, 1), (A2b, 2)):
                g.dma_start(dst[:, :], mod_d[NB:NC, src * D:(src + 1) * D].to_broadcast([P, D])).then_inc(bc_loaded, 16)
            for dst, src in ((g1s, 0), (sh2s, 1), (A2s, 2)):
                g.dma_start(dst[:, :], mod_d[0:NB, src * D:(src + 1) * D]).then_inc(bc_loaded, 16)
            g.dma_start(h2f[:, :], norm2_g.to_broadcast([P, D])).then_inc(bc_loaded, 16)
            g.dma_start(rw[:, :, :], router_w[0].rearrange("(k p) e -> p k e", p=P)).then_inc(bc_loaded, 16)
            g.dma_start(rbb[:, :], router_b.to_broadcast([P, E])).then_inc(bc_loaded, 16)
            link(g.memset(zeros[:, :], 0.0))
            for b in range(E, TASKS):
                g.dma_start(y_d[b * P:b * P + P, :].rearrange("p (a c) -> p a c", c=P),
                            zeros[:, :].unsqueeze(1).to_broadcast([P, D // P, P])).then_inc(y_zero, 16)
            g.wait_ge(chunk_used, C_MOE)
            g.memset(h2[:, TT - 1, :, :].bitcast(F32), 0.0).then_inc(h2_zero, 1)
            for t in range(TT):
                g.wait_ge(x2_done, TT + t + 1)
                g.dma_start(x2_d[t * P:t * P + ROWS[t], :], x2[0:ROWS[t], t, :]).then_inc(x2_spill, 16)
            g.wait_ge(x2_spill, 16 * TT)

            def lo_pair(s):
                for a in range(2):
                    for i in LO_POOL:
                        c = C_MOE + a * PER_TASK + i
                        g.wait_ge(hi_done, s * PER_PAIR + (split_no(c) + 1))
                        tt(w_lo[:, c % R_LO, :], raw[:, c % R_LO, :], hi_slot(c).bitcast(F32),
                           ALU.subtract).then_inc(lo_pool, 1)

            with g.Fori(0, PAIRS_MAIN) as s:
                lo_pair(s)
            g.wait_ge(tables_done, 1)
            n_pairs = g.value_load(task_i[0:1, XTRA:XTRA + 1], min_val=PAIRS_MAIN, max_val=PAIRS)
            with g.Fori(PAIRS_MAIN, PAIRS) as s:
                with g.If(s < n_pairs):
                    lo_pair(s)

            g.wait_ge(rows_ready, 1)
            for t in range(TT):
                for j in range(K):
                    if t >= 2:
                        if j == 0:
                            g.wait_ge(acc_done, t - 1)
                    g.indirect_dma_start(
                        out=yrow[0:ROWS[t], t % 2, j, :], out_offset=None, in_=y_d,
                        in_offset=bass.IndirectOffsetOnAxis(ap=rows_i[0:ROWS[t], t, j:j + 1], axis=0),
                    ).then_inc([fetched, fetched2][t % 2], 16)
                if t == 0:
                    for u in range(TT):
                        g.dma_start(x2e[0:ROWS[u], u, :], x2_d[u * P:u * P + ROWS[u], :]).then_inc(e_loaded, 16)
                    g.dma_start(g2b[:, :], mod_d[NB:NC, 3 * D:4 * D].to_broadcast([P, D])).then_inc(e_loaded, 16)
                    g.dma_start(g2s[:, :], mod_d[0:NB, 3 * D:4 * D]).then_inc(e_loaded, 16)
                    g.dma_start(fgb[:, :], final_g.rearrange("(a n) -> a n", a=1).to_broadcast([P, D]))\
                        .then_inc(e_loaded, 16)
                    g.dma_start(bdn[:, :], moe_b_down[0]).then_inc(e_loaded, 16)
            g.wait_ge(old_rows, 48)

        @block.scalar
        def _(act):
            ac = nc.scalar
            n_chain = [0]

            def link(ins):
                n_chain[0] += 1
                ins.then_inc(act_chain, 1)
                act.wait_ge(act_chain, n_chain[0])

            def hi(c, s=None):
                slot, use = c % R_LO, c // R_LO
                if s is None:
                    act.wait_ge(raw_full[slot], 16 * (use + 1))
                    if split_no(c) >= R_HI:
                        before = c - R_HI if c < C_WOUT or c >= C_WOUT + R_HI else c - R_HI - ADA_B
                        act.wait_ge(chunk_used, before + 1)
                else:
                    act.wait_ge(raw_full[slot], s * (16 * PER_PAIR // R_LO) + 16 * (use + 1))
                    act.wait_ge(chunk_used, s * PER_PAIR + (c - R_HI + 1))
                ac.activation(hi_slot(c), raw[:, slot, :], ACT.Copy).then_inc(hi_done, 1)

            act.wait_ge(c_loaded, 32)
            ac.activation(modA[0:NC, 0:D], c_all[:, :], ACT.Sigmoid).then_inc(silu_done, 1)
            def small_parameters():
                act.wait_ge(prm_ps, 1)
                link(ac.activation(prmT[:, 0:110], bk[6][:, 0:110], ACT.Copy))
                act.wait_ge(st_ps, 1)
                ac.activation(sT_pool[:, :, :].rearrange("p a b -> p (a b)"), bk[5][:, 0:240], ACT.Copy)
                ac.activation(sT_lru[:, :, :].rearrange("p a b -> p (a b)"), bk[5][:, 240:336], ACT.Copy)
                ac.activation(sT_h[:, :, :].rearrange("p a b -> p (a b)"), bk[5][:, 336:368], ACT.Copy)
                link(ac.activation(sT_conv[:, :, :].rearrange("p a b -> p (a b)"), bk[7][:, 0:480], ACT.Copy))
                link(ac.activation(cols[:, SP8:SP8 + 4], prmT[:, 77:78 + 24:8], ACT.Abs))
                ac.activation(cols[:, SP8 + 4:SP8 + 8], cols[:, SP8:SP8 + 4], ACT.Exp, scale=-1.0).then_inc(prm_done, 1)

            def squares():
                act.wait_ge(x_loaded, 32)
                act.wait_ge(consts_done, 1)
                for t in range(TT):
                    link(ac.activation(scr1[0:ROWS[t], :], x1[0:ROWS[t], t, :], ACT.Square,
                                       accum_out=cols[0:ROWS[t], SSQ + t:SSQ + t + 1]))
                ac.activation(cols[:, RSTD:RSTD + TT], cols[:, SSQ:SSQ + TT], ACT.Sqrt, scale=1.0 / D,
                              bias=cols[:, EPS:EPS + 1]).then_inc(ss1_done, 1)

            for n in range(4):
                act.wait_ge(chunk_used, 2 * n + 2)
                if n == 0:
                    act.wait_ge(cT_done, 1)
                ac.activation(modA[:, 512 * n:512 * n + 512], bk[n % 2][0:NC, :], ACT.Copy).then_inc(ada_ev, 1)
                if n == 1:
                    squares()
                if n == 3:
                    small_parameters()
            for i in range(3):
                hi(C_WIN + i)
            act.wait_ge(modT_done, 1)
            for k in range(KC):
                act.wait_ge(xT_ps, k + 1)
                if k >= 2:
                    act.wait_ge(hT_done, k - 1)
                ac.activation(hf[:, k % 2, 0:SEQ], bk[3 + k % 2], ACT.Identity, scale=mT[:, KC + k, NB:NC],
                              bias=mT[:, k, NB:NC])\
                    .then_inc(h1_act, 1)

            zi = [0]

            def z_tile():
                z_wait(act, zi[0])
                zi[0] += 1
                return pair(2 * ((zi[0] - 1) % 2))

            def gates(m):
                j = m % 2
                act.wait_ge(gates_ps, m + 1)
                link(ac.activation(two(W[:, 2 + j, :]), pair(4), ACT.Sigmoid, bias=lrp(5, m)))
                ac.activation(two(W[:, 4 + j, :]), pair(6), ACT.Sigmoid, bias=lrp(6, m)).then_inc(gates_done, 1)
                ac.activation(W[:, 2 + j, :], W[:, 2 + j, :], ACT.Tanh, scale=cols[:, SP8 + m:SP8 + m + 1])\
                    .then_inc(lru_act, 1)

            def roots(m):
                act.wait_ge(lru_dve, m + 1)
                ac.activation(W[:, 2 + m % 2, :], W[:, 2 + m % 2, :], ACT.Sqrt, scale=4.0).then_inc(lru_sqrt, 1)

            for i in range(WIN):
                if i + 3 < WIN:
                    hi(C_WIN + i + 3)
                for j in range(2):
                    tile_ = 2 * WIN_ORDER[i] + j
                    if i == 4:
                        zi[0] += 1
                        continue
                    src = z_tile()
                    if tile_ >= 10:
                        act.wait_ge(prm_done, 1)
                        ac.activation(two(g_lru[:, tile_ - 10, :]), src, ACT.Gelu_apprx_tanh).then_inc(z_ev, 1)
                    elif tile_ >= 6:
                        dst = x_lru[:, tile_ - 6, LB:LB + TOK]
                        ac.activation(two(dst), src, ACT.Copy).then_inc(z_ev, 1)
                    elif tile_ >= 4:
                        ac.activation(two(sg_conv[:, tile_ - 4, :]), src, ACT.Sigmoid).then_inc(z_ev, 1)
                    else:
                        ac.activation(two(v_conv[:, tile_ - 2, :]), src, ACT.Copy).then_inc(z_ev, 1)
                if i == 3:
                    gates(0)
                if i == 4:
                    gates(1)
                    roots(0)
                if i == 6:
                    roots(1)
            for n in range(8):
                act.wait_ge(chunk_used, C_ADAB + 2 * n + 2)
                if n:
                    act.wait_ge(mod_out, 16 * n)
                ac.activation(modst[:, :], bk[n % 2][0:NC, :], ACT.Copy).then_inc(ada_ev, 1)
                act.wait_ge(ada_ev, 5 + n)
                act.dma_start(mod_d[:, 512 * n:512 * n + 512], modst[:, :]).then_inc(mod_out, 16)
                for i in WOUT_AT.get(n, ()):
                    hi(C_WOUT + i)
                if n == 0:
                    gates(2)
                if n == 1:
                    gates(3)
                if n == 2:
                    roots(2)
                if n == 3:
                    roots(3)
                if n == 5:
                    for m in range(2):
                        act.wait_ge(centered, m + 1)
                        ac.activation(W[:, 8 + m, :], W[:, 6 + m, :], ACT.Square).then_inc(sq_done, 1)
                if n == 6:
                    act.wait_ge(ln_var, 1)
                    ac.activation(two(W[:, 8, :]), pair(6), ACT.Sqrt, scale=1.0 / D_CONV,
                                  bias=cols[:, LNEPS:LNEPS + 1]).then_inc(ln_sd, 1)
                    for m in range(2):
                        act.wait_ge(ln_pre, m + 1)
                        ac.activation(W[:, 8 + m, :], W[:, 6 + m, :], ACT.Sigmoid).then_inc(ln_sig, 1)
                if n == 7:
                    act.wait_ge(oT_done, 4)
                    for m in range(2):
                        act.wait_ge(pool_ps, m + 1)
                        ac.activation(two(W[:, m, :]), pair(4 + 2 * m), ACT.Copy, scale=cvp(34, m))\
                            .then_inc(pool_in, 1)
            act.wait_ge(tail_ps, 1)
            act.wait_ge(o_split, 4)
            ac.activation(tail[0:23, 0:256], bk[0][0:23, 0:256], ACT.Copy)
            ac.activation(tail[0:38, 256:512], bk[0][0:38, 256:512], ACT.Copy)
            ac.activation(tail[0:11, 512:1024], bk[1][0:11, :], ACT.Copy)
            ac.activation(tail[0:9, 1024:1536], bk[2][0:9, :], ACT.Copy).then_inc(tail_read, 1)
            act.wait_ge(tail_read, 1)
            for dst, src in ((pool_p[0, 0], tail[0:15, 0:256]), (pool_s[0, :, PB - 1, :], tail[15:23, 0:256]),
                             (conv_p[0, 0], tail[0:30, 256:512]), (conv_s[0, :, CB - 1, :], tail[30:38, 256:512]),
                             (lruc_p[0, 0], tail[0:3, 512:1024]), (lruc_s[0, :, LB - 1, :], tail[3:11, 512:1024]),
                             (lruh_p[0], tail[0:1, 1024:1536]), (lruh_s[0], tail[1:9, 1024:1536])):
                act.dma_start(dst, src).then_inc(tail_out, 16)

            def sq2(t, n):
                r = ROWS[t]
                act.wait_ge(x2_done, TT * n + t + 1)
                link(ac.activation(sq2t[0:r, :], x2[0:r, t, 512 * n:512 * n + 512], ACT.Square,
                                   accum_out=cols[0:r, SSQ2 + 2 * t + n:SSQ2 + 2 * t + n + 1]))
            hi(C_MOE)
            for t in range(TT):
                sq2(t, 0)
            hi(C_MOE + 1)
            hi(C_MOE + 2)
            for t in range(TT):
                r = ROWS[t]
                sq2(t, 1)
                c2 = SSQ2 + 2 * t
                link(ac.activation(cols[0:r, c2:c2 + 1], cols[0:r, c2:c2 + 1], ACT.Identity,
                                   bias=cols[0:r, c2 + 1:c2 + 2]))
                ac.activation(cols[0:r, SD2 + t:SD2 + t + 1], cols[0:r, c2:c2 + 1], ACT.Sqrt, scale=1.0 / D,
                              bias=cols[0:r, EPS:EPS + 1]).then_inc(sd2_done, 1)
                act.wait_ge(h2_ready, t + 1)
                act.wait_ge(chunk_used, C_MOE)
                if t == TT - 1:
                    act.wait_ge(h2_zero, 1)
                ac.activation(h2[0:r, t, 0, :], h2f[0:r, :], ACT.Copy).then_inc(h2hi_done, 1)
                act.wait_ge(h2T_ps, t + 1)
                if t:
                    act.wait_ge(logit_ps, t)
                ac.activation(h2T[:, :, 0:r], psum[:, 2:4, :].rearrange("p a (k r) -> p (a k) r", k=4)[:, :, 0:r],
                              ACT.Copy).then_inc(h2T_done, 1)
            act.wait_ge(exp_in, 1)
            ac.activation(wts[:, :, :], wts[:, :, :], ACT.Exp).then_inc(exp_done, 1)

            def gather_even(s):
                for k in range(0, KC, 2):
                    act.wait_ge(xg_ps, s * KC + (k + 1))
                    ac.activation(xg[:, k, :, :].rearrange("p a b -> p (a b)"), bk[6], ACT.Copy).then_inc(xg_a, 1)

            def y_even(s, a):
                act.wait_ge(chunk_used, s * PER_PAIR + (C_MOE + a * PER_TASK - 1))
                b = 1 - a
                if not isinstance(s, int):
                    act.wait_ge(y_out[b], s * 16)
                ac.activation(yst[:, b, 0:512], bk[4], ACT.Copy).then_inc(y_a, 1)

            def y_send(s, a):
                act.wait_ge(y_v, s * 2 + a)
                act.wait_ge(y_a, s * 2 + a)
                b = 1 - a
                row = (s * 2 + (a - 1)) * P
                dst = y_d[row:row + P, :] if isinstance(s, int) else y_d[bass.ds(row, P), :]
                act.dma_start(dst, yst[:, b, :]).then_inc(y_out[b], 16)

            def task(s, a, first=False):
                c = C_MOE + a * PER_TASK
                t4 = s * 4 + 2 * a
                if not first:
                    hi(c + 0, s), hi(c + 1, s)
                    y_even(s, a)
                    hi(c + 2, s)
                hi(c + 3, s), hi(c + 4, s)
                if not first:
                    y_send(s, a)
                hi(c + 5, s), hi(c + 6, s)
                for h in range(2):
                    act.wait_ge(tg_done, t4 + (h + 1))
                    ac.activation(sig[:, h, :], t_g[:, h, :], ACT.Sigmoid, scale=1.702).then_inc(sig_done, 1)
                    if h == 0:
                        hi(c + 7, s), hi(c + 8, s)
                    else:
                        hi(c + 10, s), hi(c + 11, s)
                    act.wait_ge(aT_ps, t4 + (h + 1))
                    ac.activation(aT_hi[:, h, :, :].rearrange("p a b -> p (a b)"), bk[6 + h], ACT.Copy)\
                        .then_inc(aThi_done, 1)
                    if h == 0:
                        hi(c + 9, s)

            def pair_of_tasks(s, first=False):
                task(s, 0, first)
                task(s, 1)
                gather_even(s + 1)

            act.sem_inc(y_out[1], 16)
            gather_even(0)
            pair_of_tasks(0, True)
            with act.Fori(1, PAIRS_MAIN) as s:
                pair_of_tasks(s)
            act.wait_ge(tables_done, 1)
            act.wait_ge(y_zero, 16 * XTRA)
            n_pairs = act.value_load(task_i[0:1, XTRA:XTRA + 1], min_val=PAIRS_MAIN, max_val=PAIRS)
            with act.Fori(PAIRS_MAIN, PAIRS) as s:
                with act.If(s < n_pairs):
                    pair_of_tasks(s)
            y_even(n_pairs, 0)
            y_send(n_pairs, 0)
            act.wait_ge(y_out[0], n_pairs * 16)
            act.wait_ge(y_out[1], n_pairs * 16 + 16)
            act.sem_inc(rows_ready, 1)

            act.wait_ge(WT_ps, 1)
            act.wait_ge(rows_ready, 1)
            ac.activation(WT[:, 0:4, :].rearrange("p a b -> p (a b)"), bk[0][0:E, :], ACT.Copy)
            ac.activation(WT[:, 4, :], bk[1][0:E, 0:P], ACT.Copy).then_inc(WT_done, 1)
            for t in range(TT):
                r = ROWS[t]
                act.wait_ge(acc_done, t + 1)
                link(ac.activation(sq_e[0:r, :], acc[0:r, t % 2, :], ACT.Square,
                                   accum_out=cols[0:r, SSQ + t:SSQ + t + 1]))
                ac.activation(cols[0:r, RSTD + t:RSTD + t + 1], cols[0:r, SSQ + t:SSQ + t + 1], ACT.Sqrt,
                              scale=1.0 / D, bias=cols[0:r, EPS:EPS + 1]).then_inc(sde_done, 1)
            act.wait_ge(tail_out, 128)

        @block.vector
        def _(dve):
            v = nc.vector
            n_chain = [0]

            def mark(ins):
                n_chain[0] += 1
                ins.then_inc(dve_chain, 1)
                return n_chain[0]

            def link(ins):
                dve.wait_ge(dve_chain, mark(ins))

            def lo(c, s=None):
                if s is None:
                    dve.wait_ge(hi_done, split_no(c) + 1)
                else:
                    dve.wait_ge(hi_done, s * PER_PAIR + (split_no(c) + 1))
                v.tensor_tensor(w_lo[:, c % R_LO, :], raw[:, c % R_LO, :], hi_slot(c).bitcast(F32),
                                ALU.subtract).then_inc(lo_done, 1)

            dve.wait_ge(silu_done, 1)
            v.tensor_tensor(c_all[:, :], c_all[:, :], modA[0:NC, 0:D], ALU.mult).then_inc(cT_ps, 1)
            dve.wait_ge(cT_ps, 2)
            src = bk[4][:, 0:KC * NC].rearrange("p (k c) -> p k c", k=KC)
            v.tensor_copy(cT[:, :, :], src).then_inc(cT_done, 1)
            dve.wait_ge(bias_loaded, 64)
            link(v.memset(btab[:, :].bitcast(F32), 0.0))
            link(v.tensor_copy(btab[0:2 * E, :], bias_raw[:, :]))
            link(v.tensor_tensor(btab[E:2 * E, :], bias_raw[E:2 * E, :], btab[E:2 * E, :].bitcast(F32), ALU.subtract))
            dve.wait_ge(ss1_done, 1)
            link(v.reciprocal(cols[:, RSTD:RSTD + TT], cols[:, RSTD:RSTD + TT]))
            for t in range(TT):
                r = ROWS[t]
                v.tensor_scalar(x1[0:r, t, :], x1[0:r, t, :], cols[0:r, RSTD + t:RSTD + t + 1], None, ALU.mult)\
                    .then_inc(xn_done, 1)
            for i in range(3):
                lo(C_WIN + i)
            dve.wait_ge(prm_done, 1)
            dve.wait_ge(modT_ps, 1)
            link(v.tensor_copy(mT[:, :, :], bk[2][:, 0:16 * NC].rearrange("p (a c) -> p a c", a=16)))
            link(v.tensor_scalar(mT[:, 8:16, :], mT[:, 8:16, :], 1.0, None, ALU.add))
            v.tensor_tensor(mT[:, 8:16, :], mT[:, 8:16, :], prmT[:, N1G:N1G + 8].unsqueeze(2).to_broadcast([P, 8, NC]),
                            ALU.mult).then_inc(modT_done, 1)
            dve.wait_ge(modT_done, 1)
            dve.wait_ge(xs_ps, 1)
            link(v.tensor_tensor(hs[:, :, :], bk[5][:, 0:KC * NB].rearrange("p (k b) -> p k b", k=KC),
                                 mT[:, 8:16, 0:NB], ALU.mult))
            link(v.tensor_tensor(hs[:, :, :], hs[:, :, :], mT[:, 0:8, 0:NB], ALU.add))
            link(v.tensor_copy(hT_hi[:, :, SEQ:TOK], hs[:, :, :]))
            link(v.tensor_tensor(hT_lo[:, :, SEQ:TOK], hs[:, :, :], hT_hi[:, :, SEQ:TOK].bitcast(F32), ALU.subtract))
            for k in range(KC):
                dve.wait_ge(h1_act, k + 1)
                link(v.tensor_copy(hT_hi[:, k, 0:SEQ], hf[:, k % 2, 0:SEQ]))
                v.tensor_tensor(hT_lo[:, k, 0:SEQ], hf[:, k % 2, 0:SEQ], hT_hi[:, k, 0:SEQ].bitcast(F32),
                                ALU.subtract).then_inc(hT_done, 1)

            u, w1, w2, w3 = (cols[:, SP8 + 4 * i:SP8 + 4 * i + 4] for i in (1, 2, 3, 0))
            link(v.tensor_scalar(w1, u, 2.0, None, ALU.add))
            link(v.reciprocal(w1, w1))
            link(v.tensor_tensor(u, u, w1, ALU.mult))
            link(v.tensor_tensor(w1, u, u, ALU.mult))
            link(v.tensor_scalar(w2, w1, 1.0 / 13, 1.0 / 11, ALU.mult, ALU.add))
            for kk in (9, 7, 5, 3, 1):
                link(v.tensor_tensor(w2, w2, w1, ALU.mult))
                link(v.tensor_scalar(w2, w2, 1.0 / kk, None, ALU.add))
            link(v.tensor_tensor(u, u, w2, ALU.mult))
            link(v.tensor_scalar(w2, prmT[:, 77:78 + 24:8], -1.0, 0.0, ALU.mult, ALU.max))
            link(v.scalar_tensor_tensor(w3, u, 2.0, w2, ALU.mult, ALU.add))
            link(v.tensor_scalar(w3, w3, 4.0, None, ALU.mult))
            for m in range(2):
                link(v.tensor_scalar(rc16[:, m, :], iota1[:, 0:16], cols[:, WCOL + 2 + m:WCOL + 3 + m], None, ALU.min))
                link(v.reciprocal(rc16[:, m, :], rc16[:, m, :]))
            def short_conv(m):
                dve.wait_ge(z_ev, m + 5)
                if m >= 2:
                    dve.wait_ge(oT_done, m - 1)
                o = W[:, m % 2, :]
                S = sT_lru[:, m, :].rearrange("p (b r) -> p b r", b=NB)
                link(v.tensor_scalar(o[:, 0:SEQ], x_lru[:, m, 0:SEQ], lrp(0, m), lrp(4, m), ALU.mult, ALU.add))
                link(v.tensor_scalar(o[:, SEQ:TOK], S[:, :, 0], lrp(0, m), lrp(4, m), ALU.mult, ALU.add))
                for k in range(1, LW):
                    link(v.scalar_tensor_tensor(o[:, 0:SEQ], x_lru[:, m, k:k + SEQ], lrp(k, m), o[:, 0:SEQ],
                                                ALU.mult, ALU.add))
                    sam = S[:, :, k] if k < LB else x_lru[:, m, LB + SEQ:LB + TOK]
                    ins = v.scalar_tensor_tensor(o[:, SEQ:TOK], sam, lrp(k, m), o[:, SEQ:TOK], ALU.mult, ALU.add)
                    if k < LW - 1:
                        link(ins)
                ins.then_inc(xc_done, 1)

            def before_root(m):
                xc, q, ii = (W[:, 2 * b + m % 2, :] for b in range(3))
                dve.wait_ge(lru_act, m + 1)
                dve.wait_ge(gates_done, m + 1)
                link(v.tensor_tensor(ii, ii, xc, ALU.mult))
                link(v.tensor_copy(cols[:, SAVE + m % 2:SAVE + m % 2 + 1], ii[:, 0:1]))
                k = mark(v.tensor_scalar(xc, q, 1.0, None, ALU.add))
                dve.wait_ge(dve_chain, k)
                v.reciprocal(xc, xc).then_inc(lru_dve, 1)
                dve.wait_ge(lru_dve, m + 1)
                link(v.tensor_tensor(ii, ii, xc, ALU.mult))
                link(v.tensor_scalar(xc, xc, 2.0, -1.0, ALU.mult, ALU.add))

            def after_root(m):
                xc, q, ii = (W[:, 2 * b + m % 2, :] for b in range(3))
                dve.wait_ge(lru_sqrt, m + 1)
                link(v.tensor_tensor(ii, ii, q, ALU.mult))
                link(v.tensor_copy(ii[:, 0:1], cols[:, SAVE + m % 2:SAVE + m % 2 + 1]))
                link(v.tensor_tensor_scan(q[:, 0:SEQ], xc[:, 0:SEQ], ii[:, 0:SEQ], 0.0, ALU.mult, ALU.add))
                link(v.tensor_tensor(q[:, SEQ:TOK], xc[:, SEQ:TOK], sT_h[:, m, :], ALU.mult))
                link(v.tensor_tensor(q[:, SEQ:TOK], q[:, SEQ:TOK], ii[:, SEQ:TOK], ALU.add))
                v.tensor_copy(h_tail[:, m, :], q[:, SEQ - 1:TOK]).then_inc(mix_done, 1)

            taps = [0]
            last = [0, 0]

            def conv_taps(n):
                for k in range(taps[0], min(taps[0] + n, CW)):
                    for m in range(2):
                        o = W[:, 6 + m, 0:SEQ]
                        if k == 0:
                            ins = v.tensor_scalar(o, a_conv[:, m, 0:SEQ], cvp(0, m), cvp(31, m), ALU.mult, ALU.add)
                        else:
                            dve.wait_ge(dve_chain, last[m])
                            ins = v.scalar_tensor_tensor(o, a_conv[:, m, k:k + SEQ], cvp(k, m), o, ALU.mult, ALU.add)
                        last[m] = mark(ins)
                taps[0] += n

            for i in range(WIN):
                if i + 3 < WIN:
                    lo(C_WIN + i + 3)
                if i == 1:
                    dve.wait_ge(pads_done, 1)
                    dve.wait_ge(z_ev, 4)
                    v.tensor_tensor(a_conv[:, :, CB:CB + TOK], v_conv[:, :, :], sg_conv[:, :, :], ALU.mult)\
                        .then_inc(mix_done, 1)
                    dve.wait_ge(mix_done, 1)
                if i == 2:
                    conv_taps(3)
                    short_conv(0)
                if i == 3:
                    conv_taps(3)
                    short_conv(1)
                    conv_taps(3)
                if i == 4:
                    for j in range(2):
                        z_wait(dve, 8 + j)
                        S = sT_pool[:, j, :].rearrange("p (b r) -> p b r", b=NB)
                        link(v.tensor_copy(two(u_pool[:, j, PB:PB + TOK]), pair(2 * (j % 2))))
                        for q, w in ((slice(0, 64), (2, 8)[j]), (slice(64, P), (4, 16)[j])):
                            link(v.tensor_reduce(win_s[q, j, :], S[q, :, PB - (w - 1):PB], AX.X, ALU.add))
                        v.tensor_tensor(win_s[:, j, :], win_s[:, j, :], u_pool[:, j, PB + SEQ:PB + TOK], ALU.add)\
                            .then_inc(u_ev, 1)
                    conv_taps(2)
                    before_root(0)
                if i == 5:
                    before_root(1)
                    conv_taps(4)
                if i == 6:
                    after_root(0)
                    after_root(1)
                    conv_taps(4)
            def conv_samples():
                for m in range(2):
                    S = sT_conv[:, m, :].rearrange("p (b r) -> p b r", b=NB)
                    wv = prmT[:, 35 * m:35 * m + CB].unsqueeze(1).to_broadcast([P, NB, CB])
                    tmp = W[:, 8, 0:NB * CB].rearrange("p (b r) -> p b r", b=NB)
                    o = W[:, 6 + m, SEQ:TOK]
                    link(v.tensor_tensor(tmp, S, wv, ALU.mult))
                    link(v.tensor_reduce(o, tmp, AX.X, ALU.add))
                    link(v.scalar_tensor_tensor(o, a_conv[:, m, CB + SEQ:CB + TOK], cvp(30, m), o, ALU.mult, ALU.add))
                    v.tensor_scalar(o, o, cvp(31, m), None, ALU.add).then_inc(conv_done, 1)
                    dve.wait_ge(conv_done, m + 1)

            def center():
                dve.wait_ge(mu_ps, 1)
                for m in range(2):
                    v.scalar_tensor_tensor(two(W[:, 6 + m, :]), pair(4), -1.0 / D_CONV, two(W[:, 6 + m, :]),
                                           ALU.mult, ALU.add).then_inc(centered, 1)

            def normalize():
                dve.wait_ge(centered, 2)
                dve.wait_ge(ln_sd, 1)
                link(v.reciprocal(W[:, 8, :], W[:, 8, :]))
                for m in range(2):
                    link(v.tensor_tensor(W[:, 6 + m, :], W[:, 6 + m, :], W[:, 8, :], ALU.mult))
                for m in range(2):
                    v.tensor_scalar(W[:, 6 + m, :], W[:, 6 + m, :], cvp(32, m), cvp(33, m), ALU.mult, ALU.add)\
                        .then_inc(ln_pre, 1)

            def split_conv():
                for m in range(2):
                    dve.wait_ge(ln_sig, m + 1)
                    link(v.tensor_tensor(W[:, 6 + m, :], W[:, 6 + m, :], W[:, 8 + m, :], ALU.mult))
                    link(v.tensor_copy(oT_hi[:, 2 + m, :], W[:, 6 + m, :]))
                    v.tensor_tensor(oT_lo[:, 2 + m, :], W[:, 6 + m, :], oT_hi[:, 2 + m, :].bitcast(F32), ALU.subtract)\
                        .then_inc(o_split, 1)

            def split_pool():
                for m in range(2):
                    dve.wait_ge(pool_in, m + 1)
                    link(v.tensor_copy(oT_hi[:, m, :], W[:, m, :]))
                    v.tensor_tensor(oT_lo[:, m, :], W[:, m, :], oT_hi[:, m, :].bitcast(F32), ALU.subtract)\
                        .then_inc(o_split, 1)

            for n in range(8):
                for i in WOUT_AT.get(n, ()):
                    lo(C_WOUT + i)
                if n == 0:
                    short_conv(2)
                    short_conv(3)
                    conv_taps(2)
                if n == 1:
                    before_root(2)
                    conv_taps(3)
                if n == 2:
                    before_root(3)
                    conv_taps(3)
                    conv_taps(CW)
                if n == 3:
                    after_root(2)
                    after_root(3)
                    conv_samples()
                if n == 5:
                    center()
                if n == 6:
                    normalize()
                if n == 7:
                    split_conv()
            split_pool()

            dve.wait_ge(x2_loaded, 32)
            dve.wait_ge(bc_loaded, 16 * BC_LOADS)
            link(v.tensor_scalar(A2s[:, :], A2s[:, :], 1.0, None, ALU.add))
            link(v.tensor_scalar(A2b[:, :], A2b[:, :], 1.0, None, ALU.add))
            link(v.tensor_tensor(A2s[:, :], A2s[:, :], h2f[0:NB, :], ALU.mult))
            link(v.tensor_tensor(A2b[:, :], A2b[:, :], h2f[:, :], ALU.mult))

            def residual(t, n):
                r, q = ROWS[t], slice(512 * n, 512 * n + 512)
                g1 = g1b if t < TT - 1 else g1s
                wo_wait(dve, n, t)
                b = (TT * n + t) % 8
                if n or t:
                    dve.wait_ge(x2_done, TT * n + t)
                link(v.tensor_tensor(h2f[0:r, q], bk[b][0:r, :], g1[0:r, q], ALU.mult))
                v.tensor_tensor(x2[0:r, t, q], x2[0:r, t, q], h2f[0:r, q], ALU.add).then_inc(x2_done, 1)

            lo(C_MOE)
            for t in range(TT):
                residual(t, 0)
            lo(C_MOE + 1)
            lo(C_MOE + 2)
            for t in range(TT):
                r = ROWS[t]
                A2, sh2 = (A2b, sh2b) if t < TT - 1 else (A2s, sh2s)
                if t:
                    dve.wait_ge(h2T_ps, t)
                    dve.wait_ge(h2_done, t)
                residual(t, 1)
                sd = cols[0:r, SD2 + t:SD2 + t + 1]
                dve.wait_ge(sd2_done, t + 1)
                link(v.reciprocal(sd, sd))
                link(v.scalar_tensor_tensor(h2f[0:r, :], x2[0:r, t, :], sd, A2[0:r, :], ALU.mult, ALU.mult))
                v.tensor_tensor(h2f[0:r, :], h2f[0:r, :], sh2[0:r, :], ALU.add).then_inc(h2_ready, 1)
                dve.wait_ge(h2hi_done, t + 1)
                v.tensor_tensor(h2[0:r, t, 1, :], h2f[0:r, :], h2[0:r, t, 0, :].bitcast(F32), ALU.subtract)\
                    .then_inc(h2_done, 1)
            dve.wait_ge(h2_done, TT)

            link(v.memset(logit[:, :, :], 0.0))
            link(v.memset(pp[:, :, :], 0.0))
            dve.wait_ge(logit_ps, TT)
            for t in range(TT):
                r = ROWS[t]
                link(v.tensor_tensor(logit[0:r, t, :], bk[4][0:r, E * t:E * t + E], rbb[0:r, :], ALU.add))
            for t in range(TT):
                link(v.max(v8[:, t, :], logit[:, t, :]))
                link(v.max_index(i8[:, t, :], v8[:, t, :], logit[:, t, :]))
            link(v.tensor_tensor(wts[:, :, :], v8[:, :, 0:K], v8[:, :, 0:1].to_broadcast([P, TT, K]), ALU.subtract))
            v.tensor_copy(i8f[:, :, :], i8[:, :, :]).then_inc(exp_in, 1)
            dve.wait_ge(exp_in, 1)
            for t in range(TT):
                link(v.tensor_tensor(hot[:, t, :, :], etab[:, 0:E].unsqueeze(1).to_broadcast([P, K, E]),
                                     i8f[:, t, 0:K].unsqueeze(2).to_broadcast([P, K, E]), ALU.is_equal))
            link(v.tensor_reduce(mask[:, :, :], hot[:, :, :, :].rearrange("p t j e -> p t e j"), AX.X, ALU.add))
            v.tensor_scalar(mask[:, TT - 1, :], mask[:, TT - 1, :], tri[:, NB:NB + 1], None, ALU.mult)\
                .then_inc(pp_done, 1)
            dve.wait_ge(pp_done, 2)
            v.scalar_tensor_tensor(pp[:, :, 0:E], bk[5][:, 0:TT * E].rearrange("p (t e) -> p t e", t=TT), 1.0,
                                   mask[:, :, :], ALU.add, ALU.mult).then_inc(posT_ps, 1)
            dve.wait_ge(posT_ps, 1)

            def gather_matrix(j, s):
                e = s * 2 + j
                col = pp[:, :, e:e + 1] if isinstance(s, int) else pp[:, :, bass.ds(e, 1)]
                v.tensor_tensor(gat[:, :, j * P:j * P + P], iota1[:, :].unsqueeze(1).to_broadcast([P, TT, P]),
                                col.to_broadcast([P, TT, P]), ALU.is_equal).then_inc(gat_done, 1)

            def bias_rows(s):
                for j in range(2):
                    e = s * 2 + j
                    col = etab[:, e:e + 1] if isinstance(s, int) else etab[:, bass.ds(e, 1)]
                    v.tensor_tensor(sel[:, j, :], pmod[:, :], col.to_broadcast([P, P]), ALU.is_equal)\
                        .then_inc(sel_done, 1)

            dve.wait_ge(x2_spill, 16 * TT)
            gather_matrix(0, 0)
            gather_matrix(1, 0)
            bias_rows(0)
            dve.wait_ge(exp_done, 1)
            link(v.tensor_reduce(choice[:, :, 0:1].rearrange("p t a -> p (t a)"), wts[:, :, :], AX.X, ALU.add))
            link(v.reciprocal(choice[:, :, 0:1], choice[:, :, 0:1]))
            link(v.tensor_tensor(wts[:, :, :], wts[:, :, :], choice[:, :, 0:1].to_broadcast([P, TT, K]), ALU.mult))
            cnt, xe, base_, lowa, higha = (smallE[:, i, :] for i in range(5))
            link(v.tensor_copy(cnt, bk[5][:, TT * E:TT * E + E]))
            link(v.tensor_scalar(xe, cnt, float(P), None, ALU.is_gt))
            for b in range(2, TT):
                link(v.scalar_tensor_tensor(xe, cnt, float(P * b), xe, ALU.is_gt, ALU.add))
            link(v.tensor_tensor_scan(base_, ones[:, 0:E], xe, 0.0, ALU.mult, ALU.add))
            link(v.tensor_scalar(logit[0:1, 0, 0:8], iota1[0:1, 0:8], 2.0, -2.0, ALU.mult, ALU.add))
            link(v.tensor_tensor(logit[0:1, 0, 0:8], logit[0:1, 0, 0:8], base_[0:1, E - 1:E].to_broadcast([1, 8]),
                                 ALU.is_lt))
            link(v.tensor_reduce(extras[:, 0:1], logit[0:1, 0, 0:8], AX.X, ALU.add))
            link(v.tensor_scalar(extras[:, 0:1], extras[:, 0:1], float(PAIRS_MAIN), None, ALU.add))
            link(v.tensor_copy(task_i[:, XTRA:XTRA + 1], extras[:, 0:1]))
            link(v.tensor_tensor(base_, base_, xe, ALU.subtract))
            link(v.tensor_scalar(higha, base_, float(P), float((E - 1) * P), ALU.mult, ALU.add))
            link(v.tensor_scalar(lowa, etab[:, 0:E], float(P), None, ALU.mult))
            link(v.tensor_tensor(higha, higha, lowa, ALU.subtract))
            bc = lambda x: x.unsqueeze(1).to_broadcast([P, TT, E])
            link(v.tensor_scalar(rowm[:, :, :], pp[:, :, 0:E], float(P), None, ALU.is_gt))
            link(v.tensor_tensor(rowm[:, :, :], rowm[:, :, :], bc(higha), ALU.mult))
            link(v.tensor_tensor(rowm[:, :, :], rowm[:, :, :], bc(lowa), ALU.add))
            link(v.scalar_tensor_tensor(rowm[:, :, :], pp[:, :, 0:E], -1.0, rowm[:, :, :], ALU.add, ALU.add))
            for t in range(TT):
                h4 = hot[:, t, :, :]
                w4 = tmpE4[:, :, :]
                link(v.tensor_tensor(w4, h4, wts[:, t, :].unsqueeze(2).to_broadcast([P, K, E]), ALU.mult))
                link(v.tensor_reduce(wfull[:, t, :], w4.rearrange("p j e -> p e j"), AX.X, ALU.add))
                link(v.tensor_tensor(h4, h4, rowm[:, t, :].unsqueeze(1).to_broadcast([P, K, E]), ALU.mult))
            link(v.tensor_reduce(choice[:, :, :], hot[:, :, :, :], AX.X, ALU.add))
            link(v.tensor_copy(rows_i[:, :, :], choice[:, :, :]))
            def gather_odd(s):
                for k in range(1, KC, 2):
                    dve.wait_ge(xg_ps, s * KC + (k + 1))
                    v.tensor_copy(xg[:, k, :, :].rearrange("p a b -> p (a b)"), bk[7]).then_inc(xg_d, 1)

            gather_odd(0)
            dve.wait_ge(posT_ps, 2)
            link(v.tensor_copy(posT[:, 0:4, :].rearrange("p a b -> p (a b)"), bk[4][0:E, :]))
            link(v.tensor_copy(posT[:, 4, :], bk[3][0:E, 0:P]))
            link(v.tensor_copy(xcol[:, 0:1], bk[2][0:E, 0:1]))
            link(v.tensor_scalar(xcol[:, 1:2], xcol[:, 0:1], float(P), None, ALU.is_gt))
            for b in range(2, TT):
                link(v.scalar_tensor_tensor(xcol[:, 1:2], xcol[:, 0:1], float(P * b), xcol[:, 1:2], ALU.is_gt, ALU.add))
            v.tensor_copy(xcol[:, 2:3], xcol[:, 1:2]).then_inc(xe_done, 1)
            dve.wait_ge(base_ps, 1)
            for b in range(1, TT):
                link(v.tensor_scalar(xcol[:, 4:5], bk[1][0:E, 0:1], float(b), None, ALU.add))
                link(v.tensor_scalar(xcol[:, 5:6], xcol[:, 1:2], float(b), None, ALU.is_ge))
                link(v.tensor_scalar(selX[:, 2, :], iota1[0:E, 0:XTRA], xcol[:, 4:5], xcol[:, 5:6], ALU.is_equal,
                                     ALU.mult))
                if b == 1:
                    link(v.tensor_copy(selX[:, 0, :], selX[:, 2, :]))
                    link(v.tensor_scalar(selX[:, 1, :], selX[:, 2, :], float(-P), None, ALU.mult))
                else:
                    link(v.tensor_tensor(selX[:, 0, :], selX[:, 0, :], selX[:, 2, :], ALU.add))
                    link(v.scalar_tensor_tensor(selX[:, 1, :], selX[:, 2, :], float(-P * b), selX[:, 1, :],
                                                ALU.mult, ALU.add))
            v.tensor_copy(xcol[:, 6:7], xcol[:, 1:2]).then_inc(selX_done, 1)
            dve.wait_ge(xtab_ps, 1)
            link(v.tensor_copy(pp[:, :, E:TASKS], bk[0][:, 0:TT * XTRA].rearrange("p (t q) -> p t q", t=TT)))
            link(v.tensor_copy(etab[:, E:TASKS], bk[0][:, TT * XTRA:TT * XTRA + XTRA]))
            v.tensor_copy(task_i[:, 0:XTRA], etab[0:1, E:TASKS]).then_inc(tables_done, 1)
            dve.wait_ge(tables_done, 1)

            def y_odd(s, a):
                dve.wait_ge(chunk_used, s * PER_PAIR + (C_MOE + a * PER_TASK))
                dve.wait_ge(y_a, s * 2 + a)
                v.tensor_copy(yst[:, 1 - a, 512:D], bk[5]).then_inc(y_v, 1)

            def glu(s, a, h):
                t4 = s * 4 + 2 * a
                c8 = s * 8 + (4 * a + 2 * h)
                v.tensor_scalar(ucl[:, h, :], bk[2 * h + 1], 7.0, -7.0, ALU.min, ALU.max).then_inc(moe_chain, 1)
                dve.wait_ge(moe_chain, c8 + 1)
                v.scalar_tensor_tensor(ucl[:, h, :], ucl[:, h, :], 1.0, t_g[:, h, :], ALU.add, ALU.mult)\
                    .then_inc(moe_chain, 1)
                dve.wait_ge(moe_chain, c8 + 2)
                dve.wait_ge(sig_done, t4 + (h + 1))
                v.tensor_tensor(actv[:, h, :], ucl[:, h, :], sig[:, h, :], ALU.mult).then_inc(act_done, 1)

            def turned_lo(s, a, h):
                dve.wait_ge(aThi_done, s * 4 + (2 * a + h + 1))
                v.tensor_tensor(aT_lo[:, h, :, :].rearrange("p a b -> p (a b)"), bk[6 + h],
                                aT_hi[:, h, :, :].rearrange("p a b -> p (a b)").bitcast(F32), ALU.subtract)\
                    .then_inc(aTlo_done, 1)

            def task(s, a, first=False):
                c = C_MOE + a * PER_TASK

                def split(*chunks):
                    for i in chunks:
                        if i not in LO_POOL:
                            lo(c + i, s)

                if not first:
                    split(0, 1, 2)
                    y_odd(s, a)
                if a == 0:
                    dve.wait_ge(xg_ps, s * KC + KC)
                    gather_matrix(0, s + 1)
                    gather_matrix(1, s + 1)
                split(3, 4, 5)
                dve.wait_ge(chunk_used, s * PER_PAIR + (c + 2))
                v.tensor_scalar(t_g[:, 0, :], bk[0], 7.0, None, ALU.min).then_inc(tg_done, 1)
                split(6)
                dve.wait_ge(tg_done, s * 4 + (2 * a + 1))
                dve.wait_ge(chunk_used, s * PER_PAIR + (c + 4))
                glu(s, a, 0)
                split(7, 8)
                turned_lo(s, a, 0)
                dve.wait_ge(chunk_used, s * PER_PAIR + (c + 6))
                v.tensor_scalar(t_g[:, 1, :], bk[2], 7.0, None, ALU.min).then_inc(tg_done, 1)
                split(9)
                dve.wait_ge(tg_done, s * 4 + (2 * a + 2))
                dve.wait_ge(chunk_used, s * PER_PAIR + (c + 8))
                glu(s, a, 1)
                if a == 1:
                    bias_rows(s + 1)
                split(10)
                turned_lo(s, a, 1)
                split(11)

            def pair_of_tasks(s, first=False):
                task(s, 0, first)
                task(s, 1)
                gather_odd(s + 1)

            pair_of_tasks(0, True)
            with dve.Fori(1, PAIRS_MAIN) as s:
                pair_of_tasks(s)
            n_pairs = dve.value_load(task_i[0:1, XTRA:XTRA + 1], min_val=PAIRS_MAIN, max_val=PAIRS)
            with dve.Fori(PAIRS_MAIN, PAIRS) as s:
                with dve.If(s < n_pairs):
                    pair_of_tasks(s)
            y_odd(n_pairs, 0)

            dve.wait_ge(e_loaded, 16 * (TT + 4))
            for t in range(TT):
                r, b = ROWS[t], t % 2
                g2 = g2b if t < TT - 1 else g2s
                A = acc[0:r, b, :]
                dve.wait_ge([fetched, fetched2][b], 16 * K * (t // 2 + 1))
                dve.wait_ge(yb_ps, t + 1)
                for j in range(K):
                    for n in range(2):
                        q = slice(512 * n, 512 * n + 512)
                        other = bk[2 + 2 * b + n][0:r, :] if j == 0 else A[:, q]
                        ins = v.scalar_tensor_tensor(A[:, q], yrow[0:r, b, j, q], wts[0:r, t, j:j + 1], other,
                                                     ALU.mult, ALU.add)
                        if n == 1:
                            link(ins)
                link(v.tensor_tensor(A, A, g2[0:r, :], ALU.mult))
                v.tensor_tensor(A, A, x2e[0:r, t, :], ALU.add).then_inc(acc_done, 1)
                dve.wait_ge(sde_done, t + 1)
                rs = cols[0:r, RSTD + t:RSTD + t + 1]
                link(v.reciprocal(rs, rs))
                if t >= 2:
                    dve.wait_ge([out_sent, out_sent2][b], 16 * (t // 2))
                v.scalar_tensor_tensor(out_t[0:r, b, :], A, rs, fgb[0:r, :], ALU.mult, ALU.mult)\
                    .then_inc(out_ready, 1)

        @block.tensor
        def _(pe):
            mm = nc.tensor.matmul

            def three(out, lhi, llo, rhi, rlo, start, stop):
                mm(out, lhi, rhi, start=start, stop=False)
                mm(out, lhi, rlo, start=False, stop=False)
                return mm(out, llo, rhi, start=False, stop=stop)

            def turn(out, src, rows):
                return nc.tensor.transpose(out, src, ident[0:rows, 0:rows])

            pe.wait_ge(consts_done, 1)
            pe.wait_ge(cT_ps, 1)
            for k in range(KC):
                last = turn(bk[4][:, NC * k:NC * k + NC], c_all[:, k * P:k * P + P], NC)
            last.then_inc(cT_ps, 1)
            def small_parameters():
                pe.wait_ge(prm_loaded, 16 * PRM_LOADS)
                for m in range(2):
                    turn(bk[6][:, 35 * m:35 * m + 35], cv[:, m * P:m * P + P], 35)
                for m in range(4):
                    turn(bk[6][:, 70 + 8 * m:78 + 8 * m], lr[:, m * P:m * P + P], 8)
                for k in range(KC):
                    last = turn(bk[6][:, N1G + k:N1G + k + 1], ng[:, k * P:k * P + P], 1)
                last.then_inc(prm_ps, 1)
                for m in range(2):
                    turn(bk[5][:, 120 * m:120 * m + 120], st_pool[:, m * P:m * P + P], 120)
                for m in range(4):
                    turn(bk[5][:, 240 + 24 * m:264 + 24 * m], st_lru[:, m * P:m * P + P], 24)
                    turn(bk[5][:, 336 + 8 * m:344 + 8 * m], st_h[:, m * P:m * P + P], 8)
                for m in range(2):
                    for a in range(2):
                        last = turn(bk[7][:, 240 * m + 120 * a:240 * m + 120 * a + 120],
                                    st_conv[:, a, m * P:m * P + P], 120)
                last.then_inc(st_ps, 1)

            def chunk(c):
                pe.wait_ge(lo_done, split_no(c) + 1)
                return hi_slot(c), w_lo[:, c % R_LO, :]

            def ada_block(n, c):
                out = bk[n % 2][0:NC, :]
                if n == 0:
                    pe.wait_ge(cT_done, 1)
                if 2 <= n < 4 or n >= 6:
                    pe.wait_ge(ada_ev, n - 1)
                if n == 4:
                    pe.wait_ge(z_ev, 12)
                mm(out, bsel[:, n, :], adab[:, :], start=True, stop=False)
                for kh in range(2):
                    slot, use = (c + kh) % R_LO, (c + kh) // R_LO
                    pe.wait_ge(raw_full[slot], 16 * (use + 1))
                    for k in range(4):
                        last = mm(out, cT[:, 4 * kh + k, :], raw[:, slot, 512 * k:512 * k + 512], start=False,
                                  stop=(kh == 1 and k == 3))
                    last.then_inc(chunk_used, 1)

            pe.wait_ge(adab_loaded, 16)
            for n in range(4):
                ada_block(n, 2 * n)
            small_parameters()
            pe.wait_ge(ada_ev, 4)
            for m in range(16):
                last = turn(bk[2][:, NC * m:NC * m + NC], modA[:, m * P:m * P + P], NC)
            last.then_inc(modT_ps, 1)
            pe.wait_ge(xn_done, TT)
            pe.wait_ge(prm_done, 1)
            for k in range(KC):
                last = turn(bk[5][:, NB * k:NB * k + NB], x1[0:NB, TT - 1, k * P:k * P + P], NB)
            last.then_inc(xs_ps, 1)
            for k in range(KC):
                if k >= 2:
                    pe.wait_ge(h1_act, k - 1)
                for t in range(TT - 1):
                    last = turn(bk[3 + k % 2][:, t * P:t * P + P], x1[:, t, k * P:k * P + P], P)
                last.then_inc(xT_ps, 1)

            def z_tiles(i):
                whi, wlo = chunk(C_WIN + i)
                whi, wlo = wide(whi), wide(wlo)
                for j in range(2):
                    z = 2 * i + j
                    if z >= 2:
                        if z - 2 in (8, 9):
                            pe.wait_ge(u_ev, z - 2 - 7)
                        else:
                            pe.wait_ge(z_ev, z - 1 if z - 2 < 8 else z - 3)
                    for h in range(2):
                        out = psum[:, 2 * (z % 2) + h, 0:TOK // 2]
                        q = slice(TOK // 2 * h, TOK // 2 * h + TOK // 2)
                        for k in range(KC):
                            m = slice(P * j, P * j + P)
                            last = three(out, whi[:, k, m], wlo[:, k, m], hT_hi[:, k, q], hT_lo[:, k, q],
                                         k == 0, k == KC - 1)
                    last.then_inc(chunk_used if j else z_ps, 1)

            def channel_sums(b, w):
                for h in range(2):
                    q = slice(TOK // 2 * h, TOK // 2 * h + TOK // 2)
                    for m in range(2):
                        last = mm(psum[:, b + h, 0:TOK // 2], ones[:, :], W[:, w + m, q], start=(m == 0), stop=(m == 1))
                return last

            def gates(m):
                pe.wait_ge(xc_done, m + 1)
                if m:
                    pe.wait_ge(gates_done, m)
                for b, bd in ((4, bd_a), (6, bd_x)):
                    for h in range(2):
                        last = mm(psum[:, b + h, 0:TOK // 2], bd[:, m, :],
                                  W[:, m % 2, TOK // 2 * h:TOK // 2 * h + TOK // 2], start=True, stop=True)
                last.then_inc(gates_ps, 1)

            pe.wait_ge(hT_done, KC)
            for i in range(WIN):
                z_tiles(i)
                if i == 3:
                    gates(0)
                if i == 4:
                    gates(1)
            for n in range(8):
                ada_block(4 + n, C_ADAB + 2 * n)
                if n == 0:
                    gates(2)
                if n == 1:
                    gates(3)
                if n == 4:
                    pe.wait_ge(conv_done, 2)
                    pe.wait_ge(gates_done, 4)
                    channel_sums(4, 6).then_inc(mu_ps, 1)
                if n == 6:
                    pe.wait_ge(sq_done, 2)
                    channel_sums(6, 8).then_inc(ln_var, 1)
                if n == 7:
                    pe.wait_ge(pool_d_done, 1)
                    for m in range(2):
                        if m == 0:
                            pe.wait_ge(centered, 2)
                        else:
                            pe.wait_ge(ln_sd, 1)
                        for h in range(2):
                            last = mm(psum[:, 4 + 2 * m + h, 0:TOK // 2], bd_pool[:, m, :],
                                      v_conv[:, m, TOK // 2 * h:TOK // 2 * h + TOK // 2], start=True, stop=True)
                        last.then_inc(pool_ps, 1)
            pe.wait_ge(ada_ev, 12)
            pe.wait_ge(mix_done, 5)
            for m in range(2):
                turn(bk[0][0:23, m * P:m * P + P], u_pool[:, m, PB + SEQ - PB:PB + TOK], P)
                turn(bk[0][0:38, 256 + m * P:256 + m * P + P], a_conv[:, m, CB + SEQ - CB:CB + TOK], P)
            for m in range(4):
                turn(bk[1][0:11, m * P:m * P + P], x_lru[:, m, LB + SEQ - LB:LB + TOK], P)
                last = turn(bk[2][0:9, m * P:m * P + P], h_tail[:, m, :], P)
            last.then_inc(tail_ps, 1)

            pe.wait_ge(o_split, 4)
            pe.wait_ge(oT_done, 4)
            pe.wait_ge(pool_in, 2)
            pe.wait_ge(tail_read, 1)
            for n in range(2):
                for kh in range(2):
                    whi, wlo = chunk(C_WOUT + 2 * n + kh)
                    for t in range(TT):
                        r = ROWS[t]
                        b = (TT * n + t) % 8
                        if n == 1 and kh == 0 and TT + t >= 8:
                            pe.wait_ge(x2_done, TT + t - 7)
                        for k in range(4):
                            q = slice(512 * k, 512 * k + 512)
                            kk = 4 * kh + k
                            last = three(bk[b][0:r, :], oT_hi[:, kk, t * P:t * P + r], oT_lo[:, kk, t * P:t * P + r],
                                         whi[:, q], wlo[:, q], kk == 0, kk == KC - 1)
                        if t == TT - 1:
                            last.then_inc(chunk_used, 1)
                        elif kh == 1:
                            last.then_inc(wo_ps, 1)
            for t in range(TT):
                r = ROWS[t]
                pe.wait_ge(h2_ready, t + 1)
                if t:
                    pe.wait_ge(h2T_done, t)
                for k in range(KC):
                    last = turn(psum[:, 2 + k // 4, (k % 4) * P:(k % 4) * P + r], h2f[0:r, k * P:k * P + P], r)
                last.then_inc(h2T_ps, 1)
                pe.wait_ge(h2T_done, t + 1)
                for k in range(KC):
                    last = mm(bk[4][0:r, E * t:E * t + E], h2T[:, k, 0:r], rw[:, k, :], start=(k == 0),
                              stop=(k == KC - 1))
                last.then_inc(logit_ps, 1)
            pe.wait_ge(pp_done, 1)
            for t in range(TT):
                for b in range(t):
                    mm(bk[5][:, E * t:E * t + E], ones[:, :], mask[:, b, :], start=(b == 0), stop=False)
                mm(bk[5][:, E * t:E * t + E], tri[:, :], mask[:, t, :], start=(t == 0), stop=True)
            for b in range(TT):
                last = mm(bk[5][:, E * TT:E * TT + E], ones[:, :], mask[:, b, :], start=(b == 0), stop=(b == TT - 1))
            last.then_inc(pp_done, 1)

            def gather(s, turned=None):
                for k in range(KC):
                    b = 6 + k % 2
                    if k == 1 and turned is not None:
                        pe.wait_ge(aTlo_done, turned)
                    if k >= 2:
                        if k % 2 == 0:
                            pe.wait_ge(xg_a, s * 4 + k // 2)
                        else:
                            pe.wait_ge(xg_d, s * 4 + k // 2)
                    for hl in range(2):
                        for t in range(TT):
                            last = mm(bk[b][:, 2 * P * hl:2 * P * hl + 2 * P], h2[:, t, hl, k * P:k * P + P],
                                      gat[:, t, :], start=(t == 0), stop=(t == TT - 1))
                    last.then_inc(xg_ps, 1)

            pe.wait_ge(h2_done, TT)
            pe.wait_ge(gat_done, 2)
            gather(0)
            for t in range(TT):
                out = bk[4][0:E, t * P:t * P + P] if t < 4 else bk[3][0:E, 0:P]
                turn(out, pp[:, t, 0:E], P)
            for b in range(TT):
                last = mm(bk[2][0:E, 0:1], mask[:, b, :], ones[:, 0:1], start=(b == 0), stop=(b == TT - 1))
            last.then_inc(posT_ps, 1)
            pe.wait_ge(xe_done, 1)
            mm(bk[1][0:E, 0:1], tri[0:E, 0:E], xcol[:, 2:3], start=True, stop=True).then_inc(base_ps, 1)
            pe.wait_ge(selX_done, 1)
            for t in range(TT):
                mm(bk[0][:, XTRA * t:XTRA * t + XTRA], posT[:, t, :], selX[:, 0, :], start=True, stop=False)
                mm(bk[0][:, XTRA * t:XTRA * t + XTRA], ones[0:E, :], selX[:, 1, :], start=False, stop=True)
            mm(bk[0][:, XTRA * TT:XTRA * TT + XTRA], pmod[0:E, :], selX[:, 0, :], start=True, stop=True)\
                .then_inc(xtab_ps, 1)
            pe.wait_ge(tables_done, 1)

            def moe_chunk(s, c):
                lo_wait(pe, s, c)
                return hi_slot(c), w_lo[:, c % R_LO, :]

            def task(s, a):
                c0 = C_MOE + a * PER_TASK
                t2 = s * 2 + a
                t4 = s * 4 + 2 * a
                if a == 0:
                    pe.wait_ge(xg_a, s * 4 + 4)
                    pe.wait_ge(xg_d, s * 4 + 4)
                    pe.wait_ge(sel_done, s * 2 + 2)

                def proj(b, off, mat, n):
                    mm(bk[b], sel[:, a, :], btab[:, DFF * mat + 512 * n:DFF * mat + 512 * n + 512],
                       start=True, stop=False)
                    for kh in range(2):
                        whi, wlo = moe_chunk(s, c0 + off + kh)
                        for k in range(4):
                            q = slice(512 * k, 512 * k + 512)
                            x = xg[:, 4 * kh + k, :, a * P:a * P + P]
                            last = three(bk[b], x[:, 0, :], x[:, 1, :], whi[:, q], wlo[:, q], False,
                                         kh == 1 and k == 3)
                        last.then_inc(chunk_used, 1)

                def turned(h):
                    pe.wait_ge(act_done, t4 + (h + 1))
                    for k in range(4):
                        last = turn(bk[6 + h][:, k * P:k * P + P], actv[:, h, k * P:k * P + P], P)
                    last.then_inc(aT_ps, 1)

                def down(off, kh, n):
                    whi, wlo = moe_chunk(s, c0 + off)
                    for k in range(4):
                        q = slice(512 * k, 512 * k + 512)
                        last = three(bk[4 + n], aT_hi[:, kh, k, :], aT_lo[:, kh, k, :], whi[:, q], wlo[:, q],
                                     kh == 0 and k == 0, kh == 1 and k == 3)
                    last.then_inc(chunk_used, 1)

                proj(0, 0, 0, 0)
                proj(1, 2, 1, 0)
                proj(2, 4, 0, 1)
                turned(0)
                proj(3, 6, 1, 1)
                pe.wait_ge(aTlo_done, t4 + 1)
                if not isinstance(s, int) or t2 > 0:
                    pe.wait_ge(y_a, t2)
                down(8, 0, 0)
                turned(1)
                if not isinstance(s, int) or t2 > 0:
                    pe.wait_ge(y_v, t2)
                down(9, 0, 1)
                if a == 1:
                    pe.wait_ge(gat_done, s * 2 + 4)
                    gather(s + 1, t4 + 2)
                else:
                    pe.wait_ge(aTlo_done, t4 + 2)
                down(10, 1, 0)
                down(11, 1, 1)

            def pair_of_tasks(s):
                task(s, 0)
                task(s, 1)

            pair_of_tasks(0)
            with pe.Fori(1, PAIRS_MAIN) as s:
                pair_of_tasks(s)
            n_pairs = pe.value_load(task_i[0:1, XTRA:XTRA + 1], min_val=PAIRS_MAIN, max_val=PAIRS)
            with pe.Fori(PAIRS_MAIN, PAIRS) as s:
                with pe.If(s < n_pairs):
                    pair_of_tasks(s)

            for t in range(TT):
                out = bk[0][0:E, t * P:t * P + P] if t < 4 else bk[1][0:E, 0:P]
                last = turn(out, wfull[:, t, :], P)
            last.then_inc(WT_ps, 1)
            pe.wait_ge(WT_done, 1)
            pe.wait_ge(e_loaded, 16 * (TT + 4))
            pe.wait_ge(rows_ready, 1)
            for t in range(TT):
                r = ROWS[t]
                if t >= 2:
                    pe.wait_ge(acc_done, t - 1)
                for n in range(2):
                    last = mm(bk[2 + 2 * (t % 2) + n][0:r, :], WT[:, t, 0:r], bdn[:, 512 * n:512 * n + 512],
                              start=True, stop=True)
                last.then_inc(yb_ps, 1)


_INS = ["x_prompt", "x_sample", "state_pool", "state_conv", "state_lru_conv", "state_lru_h", "c_prompt", "c_sample",
        "ada_w", "ada_b", "norm1_g", "w_in", "pool_w", "pool_scale", "conv_dw", "conv_b", "conv_ln_g", "conv_ln_b",
        "lru_conv_w", "lru_conv_b", "lru_wa", "lru_ba", "lru_wx", "lru_bx", "lru_lambda", "w_out", "norm2_g",
        "router_w", "router_b", "moe_w_gate", "moe_b_gate", "moe_w_up", "moe_b_up", "moe_w_down", "moe_b_down",
        "final_g"]
_OUTS = [(1, SEQ, D), (NB, 1, D), (1, 1, PB, D_POOL), (1, 1, CB, D_CONV), (1, 1, LB, D_LRU), (1, 1, D_LRU),
         (1, NB, PB, D_POOL), (1, NB, CB, D_CONV), (1, NB, LB, D_LRU), (1, NB, D_LRU)]


def kernel(**inputs):
    import numpy as np
    import concourse.bacc as bacc
    from concourse.bass_utils import run_bass_kernel_spmd

    nc = bacc.Bacc("TRN2", target_bir_lowering=False, num_devices=1)
    arrays, args = {}, []
    for name in _INS:
        a = np.ascontiguousarray(inputs[name])
        arrays[f"in_{name}"] = a
        args.append(nc.dram_tensor(f"in_{name}", a.shape, F32, kind="ExternalInput").ap())
    for i, shape in enumerate(_OUTS):
        args.append(nc.dram_tensor(f"out_{i}", shape, F32, kind="ExternalOutput").ap())
    trunk_program(nc, *args)
    r = run_bass_kernel_spmd(nc, [arrays], core_ids=[0])
    return tuple(r.results[0][f"out_{i}"] for i in range(len(_OUTS)))
```
